# Optimizing a Trainium2 kernel written in Bass

```python
import jax, jax.numpy as jnp
from jax import lax
import numpy as np

D_MODEL = 1024
BATCH = 1
SEQ = 512
DEPTH = 2

CTX_LEN = 256
GRID_W = 64
HEAD_DIM = 64
BLOCK = 128
MIX_W = 512
N_BRANCH = 3
A_GROUPS = 4
A_GROUP_W = MIX_W // A_GROUPS
B_HEADS = 4
B_VDIM = 2 * HEAD_DIM
C_Q_HEADS = 8
C_KV_HEADS = 2
C_GROUP = C_Q_HEADS // C_KV_HEADS
C_WINDOW = 128
D_FF = 2816
CONV_W = 3
ROPE_BASE = 10000.0
EPS = 1e-6
SCALE = HEAD_DIM ** -0.5
NEG_INF = -1e30
IN_SIZES = (MIX_W, MIX_W,
            2 * B_HEADS * HEAD_DIM, 2 * B_HEADS * HEAD_DIM,
            B_HEADS * B_VDIM,
            C_Q_HEADS * HEAD_DIM,
            C_KV_HEADS * HEAD_DIM, C_KV_HEADS * HEAD_DIM,
            N_BRANCH * D_MODEL)
IN_WIDTH = 6400

kernel_name = 'hybrid_prefix_dit_block'

def rmsnorm(x, g):
    xf = x.astype(jnp.float32)
    y = xf * lax.rsqrt(jnp.mean(xf * xf, axis=-1, keepdims=True) + EPS)
    return (y * g.astype(jnp.float32)).astype(x.dtype)

def layernorm(x, g, b):
    xf = x.astype(jnp.float32)
    mu = jnp.mean(xf, axis=-1, keepdims=True)
    var = jnp.mean(jnp.square(xf - mu), axis=-1, keepdims=True)
    y = (xf - mu) * lax.rsqrt(var + EPS)
    return (y * g.astype(jnp.float32) + b.astype(jnp.float32)).astype(x.dtype)

def ada_params(v, w, b):
    m = (jax.nn.silu(v) @ w + b)[:, None, :]
    return jnp.split(m, 6, axis=-1)

def split_cols(p):
    outs = []
    start = 0
    for size in IN_SIZES:
        outs.append(p[..., start:start + size])
        start += size
    return outs

def rope_tables(length):
    rows_n = length // GRID_W
    rows = jnp.repeat(jnp.arange(rows_n), GRID_W).astype(jnp.float32)
    cols = jnp.tile(jnp.arange(GRID_W), rows_n).astype(jnp.float32)
    half = HEAD_DIM // 2
    inv = ROPE_BASE ** (-jnp.arange(0, half, 2, dtype=jnp.float32) / half)
    ang_r = rows[:, None] * inv[None, :]
    ang_c = cols[:, None] * inv[None, :]
    return (jnp.cos(ang_r), jnp.sin(ang_r), jnp.cos(ang_c), jnp.sin(ang_c))

def _rot(xh, cos, sin):
    x1, x2 = jnp.split(xh, 2, axis=-1)
    cos = cos[None, :, None, :]
    sin = sin[None, :, None, :]
    return jnp.concatenate([x1 * cos - x2 * sin, x2 * cos + x1 * sin], axis=-1)

def apply_rope(x, tables):
    cos_r, sin_r, cos_c, sin_c = tables
    xf = x.astype(jnp.float32)
    xr, xc = jnp.split(xf, 2, axis=-1)
    return jnp.concatenate([_rot(xr, cos_r, sin_r), _rot(xc, cos_c, sin_c)], axis=-1).astype(x.dtype)

def spatial_gating(u, v, ln_g, ln_b, w_s, b_s):
    bsz, length, _ = u.shape
    u = jax.nn.gelu(u)
    vn = layernorm(jax.nn.gelu(v), ln_g, ln_b)
    vz = vn.reshape(bsz, length // BLOCK, BLOCK, A_GROUPS, A_GROUP_W)
    mixed = jnp.einsum('gpq,bnqgc->bnpgc', w_s, vz) + b_s.T[None, None, :, :, None]
    return u * mixed.reshape(bsz, length, MIX_W)

def diff_core(q, k, v, lam):
    s = jnp.einsum('bqhmd,bkhmd->bhmqk', q, k).astype(jnp.float32) * SCALE
    p = jax.nn.softmax(s, axis=-1)
    a = p[:, :, 0] - lam * p[:, :, 1]
    return jnp.einsum('bhqk,bkhe->bqhe', a.astype(v.dtype), v)

def diff_post(o, sub_g, lam_init):
    bsz, length = o.shape[:2]
    return (rmsnorm(o, sub_g) * (1.0 - lam_init)).reshape(bsz, length, MIX_W)

def diff_attention_latent(q, k, v, k_ctx, v_ctx, lam):
    bsz, length = q.shape[:2]
    n_blk = length // BLOCK
    k_all = jnp.concatenate([k, k_ctx], axis=1)
    v_all = jnp.concatenate([v, v_ctx], axis=1)
    qb = q.reshape(bsz, n_blk, BLOCK, B_HEADS, 2, HEAD_DIM).swapaxes(0, 1)
    ob = lax.map(lambda qblk: diff_core(qblk, k_all, v_all, lam), qb)
    return ob.swapaxes(0, 1).reshape(bsz, length, B_HEADS, B_VDIM)

def window_gqa_latent(q, k, v, k_ctx, v_ctx, sink):
    bsz, length = q.shape[:2]
    n_blk = length // BLOCK
    qg = q.reshape(bsz, n_blk, BLOCK, C_KV_HEADS, C_GROUP, HEAD_DIM).swapaxes(0, 1)
    pad = ((0, 0), (BLOCK, BLOCK), (0, 0), (0, 0))
    k_pad = jnp.pad(k, pad)
    v_pad = jnp.pad(v, pad)
    sink_f = sink.astype(jnp.float32).reshape(C_KV_HEADS, C_GROUP)
    n_ctx = k_ctx.shape[1]

    def block(args):
        qblk, n = args
        start = n * BLOCK
        kb = lax.dynamic_slice_in_dim(k_pad, start, 3 * BLOCK, axis=1)
        vb = lax.dynamic_slice_in_dim(v_pad, start, 3 * BLOCK, axis=1)
        qpos = start + jnp.arange(BLOCK)
        kpos = start - BLOCK + jnp.arange(3 * BLOCK)
        rel = kpos[None, :] - qpos[:, None]
        valid = (jnp.abs(rel) <= C_WINDOW) & (kpos >= 0)[None, :] & (kpos < length)[None, :]
        s_loc = jnp.einsum('bqkgd,bjkd->bkgqj', qblk, kb).astype(jnp.float32) * SCALE
        s_loc = jnp.where(valid, s_loc, NEG_INF)
        s_ctx = jnp.einsum('bqkgd,bjkd->bkgqj', qblk, k_ctx).astype(jnp.float32) * SCALE
        s_sink = jnp.broadcast_to(sink_f[None, :, :, None, None], s_loc.shape[:-1] + (1,))
        p = jax.nn.softmax(jnp.concatenate([s_loc, s_ctx, s_sink], axis=-1), axis=-1)
        p_loc = p[..., :3 * BLOCK].astype(v.dtype)
        p_ctx = p[..., 3 * BLOCK:3 * BLOCK + n_ctx].astype(v.dtype)
        return (jnp.einsum('bkgqj,bjkd->bqkgd', p_loc, vb)
                + jnp.einsum('bkgqj,bjkd->bqkgd', p_ctx, v_ctx))

    out = lax.map(block, (qg, jnp.arange(n_blk)))
    return out.swapaxes(0, 1).reshape(bsz, length, MIX_W)

def window_gqa_context(q, k, v, sink):
    bsz, length = q.shape[:2]
    sink_f = sink.astype(jnp.float32).reshape(C_KV_HEADS, C_GROUP)
    s = jnp.einsum('bqkgd,bjkd->bkgqj', q, k).astype(jnp.float32) * SCALE
    s_sink = jnp.broadcast_to(sink_f[None, :, :, None, None], s.shape[:-1] + (1,))
    p = jax.nn.softmax(jnp.concatenate([s, s_sink], axis=-1), axis=-1)[..., :-1]
    out = jnp.einsum('bkgqj,bjkd->bqkgd', p.astype(v.dtype), v)
    return out.reshape(bsz, length, MIX_W)

def merge_branches(outs, gates, w_branch, w_out):
    bsz, length = gates.shape[:2]
    g = jax.nn.sigmoid(gates.reshape(bsz, length, N_BRANCH, D_MODEL))
    y = g[:, :, 0] * (outs[0] @ w_branch[0])
    for i in range(1, N_BRANCH):
        y = y + g[:, :, i] * (outs[i] @ w_branch[i])
    return y @ w_out

def conv_ffn(h, w_gate, conv_w, conv_b, w_up, w_down):
    a = h @ w_gate
    ap = jnp.pad(a, ((0, 0), (1, 1), (0, 0)))
    a = ap[:, :-2] * conv_w[0] + ap[:, 1:-1] * conv_w[1] + ap[:, 2:] * conv_w[2] + conv_b
    return (jax.nn.silu(a) * (h @ w_up)) @ w_down

def setup_inputs(seed: int = 0) -> dict:
    key = jax.random.key(seed)
    ks = jax.random.split(key, 32)

    def nrm(k, shape, scale):
        return jax.random.normal(k, shape, jnp.float32) * scale

    D = D_MODEL
    return {
        'x': nrm(ks[0], (BATCH, SEQ, D), 1.0),
        'c': nrm(ks[1], (BATCH, D), 1.0),
        'ctx': nrm(ks[2], (BATCH, CTX_LEN, D), 1.0),
        'c_ctx': nrm(ks[3], (D,), 1.0),
        'w_ada': nrm(ks[4], (DEPTH, D, 6 * D), 0.5 * D ** -0.5),
        'b_ada': nrm(ks[5], (DEPTH, 6 * D), 0.01),
        'norm1_g': 1.0 + nrm(ks[6], (DEPTH, D), 0.02),
        'w_in': nrm(ks[7], (DEPTH, D, IN_WIDTH), D ** -0.5),
        'sgu_ln_g': 1.0 + nrm(ks[8], (DEPTH, MIX_W), 0.02),
        'sgu_ln_b': nrm(ks[9], (DEPTH, MIX_W), 0.02),
        'w_s': nrm(ks[10], (DEPTH, A_GROUPS, BLOCK, BLOCK), BLOCK ** -0.5),
        'b_s': 1.0 + nrm(ks[11], (DEPTH, A_GROUPS, BLOCK), 0.02),
        'lam_q1': nrm(ks[12], (DEPTH, HEAD_DIM), 0.1),
        'lam_k1': nrm(ks[13], (DEPTH, HEAD_DIM), 0.1),
        'lam_q2': nrm(ks[14], (DEPTH, HEAD_DIM), 0.1),
        'lam_k2': nrm(ks[15], (DEPTH, HEAD_DIM), 0.1),
        'diff_subln_g': 1.0 + nrm(ks[16], (DEPTH, B_VDIM), 0.02),
        'sinks': nrm(ks[17], (DEPTH, C_Q_HEADS), 0.5),
        'w_branch': nrm(ks[18], (DEPTH, N_BRANCH, MIX_W, D), MIX_W ** -0.5),
        'w_out': nrm(ks[19], (DEPTH, D, D), D ** -0.5),
        'norm2_g': 1.0 + nrm(ks[20], (DEPTH, D), 0.02),
        'w_gate': nrm(ks[21], (DEPTH, D, D_FF), D ** -0.5),
        'conv_w': nrm(ks[22], (DEPTH, CONV_W, D_FF), CONV_W ** -0.5),
        'conv_b': nrm(ks[23], (DEPTH, D_FF), 0.01),
        'w_up': nrm(ks[24], (DEPTH, D, D_FF), D ** -0.5),
        'w_down': nrm(ks[25], (DEPTH, D_FF, D), D_FF ** -0.5),
        'final_g': 1.0 + nrm(ks[26], (D,), 0.02),
    }

def reference(x, c, ctx, c_ctx, w_ada, b_ada, norm1_g, w_in, sgu_ln_g, sgu_ln_b, w_s, b_s,
              lam_q1, lam_k1, lam_q2, lam_k2, diff_subln_g, sinks, w_branch, w_out,
              norm2_g, w_gate, conv_w, conv_b, w_up, w_down, final_g):
    bsz, length, _ = x.shape
    n_ctx = ctx.shape[1]
    tables = rope_tables(length)
    for l in range(DEPTH):
        last = l == DEPTH - 1
        sh1, sc1, g1, sh2, sc2, g2 = ada_params(c, w_ada[l], b_ada[l])
        csh1, csc1, cg1, csh2, csc2, cg2 = ada_params(c_ctx[None, :], w_ada[l], b_ada[l])

        h = rmsnorm(x, norm1_g[l]) * (1.0 + sc1) + sh1
        hc = rmsnorm(ctx, norm1_g[l]) * (1.0 + csc1) + csh1
        a_u, a_v, b_q, b_k, b_v, c_q, c_k, c_v, gates = split_cols(h @ w_in[l])
        ca_u, ca_v, cb_q, cb_k, cb_v, cc_q, cc_k, cc_v, cgates = split_cols(hc @ w_in[l])

        o_a = spatial_gating(a_u, a_v, sgu_ln_g[l], sgu_ln_b[l], w_s[l], b_s[l])

        lam_init = 0.8 - 0.6 * float(np.exp(-0.3 * l))
        lam = (jnp.exp(jnp.sum(lam_q1[l] * lam_k1[l]).astype(jnp.float32))
               - jnp.exp(jnp.sum(lam_q2[l] * lam_k2[l]).astype(jnp.float32)) + lam_init)
        qb = apply_rope(b_q.reshape(bsz, length, 2 * B_HEADS, HEAD_DIM), tables)
        kb = apply_rope(b_k.reshape(bsz, length, 2 * B_HEADS, HEAD_DIM), tables)
        qb = qb.reshape(bsz, length, B_HEADS, 2, HEAD_DIM)
        kb = kb.reshape(bsz, length, B_HEADS, 2, HEAD_DIM)
        vb = b_v.reshape(bsz, length, B_HEADS, B_VDIM)
        cqb = cb_q.reshape(bsz, n_ctx, B_HEADS, 2, HEAD_DIM)
        ckb = cb_k.reshape(bsz, n_ctx, B_HEADS, 2, HEAD_DIM)
        cvb = cb_v.reshape(bsz, n_ctx, B_HEADS, B_VDIM)
        o_b = diff_post(diff_attention_latent(qb, kb, vb, ckb, cvb, lam), diff_subln_g[l], lam_init)

        qc = apply_rope(c_q.reshape(bsz, length, C_Q_HEADS, HEAD_DIM), tables)
        qc = qc.reshape(bsz, length, C_KV_HEADS, C_GROUP, HEAD_DIM)
        kc = apply_rope(c_k.reshape(bsz, length, C_KV_HEADS, HEAD_DIM), tables)
        vc = c_v.reshape(bsz, length, C_KV_HEADS, HEAD_DIM)
        ckc = cc_k.reshape(bsz, n_ctx, C_KV_HEADS, HEAD_DIM)
        cvc = cc_v.reshape(bsz, n_ctx, C_KV_HEADS, HEAD_DIM)
        o_c = window_gqa_latent(qc, kc, vc, ckc, cvc, sinks[l])

        x = x + g1 * merge_branches((o_a, o_b, o_c), gates, w_branch[l], w_out[l])

        if not last:
            co_a = spatial_gating(ca_u, ca_v, sgu_ln_g[l], sgu_ln_b[l], w_s[l], b_s[l])
            co_b = diff_post(diff_core(cqb, ckb, cvb, lam), diff_subln_g[l], lam_init)
            cqc = cc_q.reshape(bsz, n_ctx, C_KV_HEADS, C_GROUP, HEAD_DIM)
            co_c = window_gqa_context(cqc, ckc, cvc, sinks[l])
            ctx = ctx + cg1 * merge_branches((co_a, co_b, co_c), cgates, w_branch[l], w_out[l])

        h2 = rmsnorm(x, norm2_g[l]) * (1.0 + sc2) + sh2
        x = x + g2 * conv_ffn(h2, w_gate[l], conv_w[l], conv_b[l], w_up[l], w_down[l])
        if not last:
            hc2 = rmsnorm(ctx, norm2_g[l]) * (1.0 + csc2) + csh2
            ctx = ctx + cg2 * conv_ffn(hc2, w_gate[l], conv_w[l], conv_b[l], w_up[l], w_down[l])

    return rmsnorm(x, final_g)


_drawn_inputs = setup_inputs


def setup_inputs(seed=0):
    import zlib

    import numpy as np

    out = dict(_drawn_inputs(seed))
    spreads = {}
    factors = {'b_ada': 3.275,
     'norm1_g': 7.903,
     'sgu_ln_g': 8.0,
     'sgu_ln_b': 8.0,
     'b_s': 8.0,
     'lam_q1': 4.845,
     'lam_k1': 3.769,
     'lam_q2': 4.531,
     'lam_k2': 5.874,
     'diff_subln_g': 64.0,
     'sinks': 8.0,
     'norm2_g': 6.751,
     'conv_b': 33.701,
     'final_g': 7.788}
    for name, (base, spread) in spreads.items():
        noise = np.random.default_rng([zlib.crc32(name.encode()), seed]).standard_normal(out[name].shape)
        drawn = base * np.exp(spread * noise) if base else spread * noise
        out[name] = __import__('jax').numpy.asarray(drawn.astype(out[name].dtype))
    for name, factor in factors.items():
        out[name] = (out[name] * factor).astype(out[name].dtype)
    return out
```

```python
from contextlib import ExitStack, contextmanager

import numpy as np

import concourse.bass as bass
from concourse import mybir

P = 128
D_MODEL, SEQ, CTX, DEPTH = 1024, 512, 256, 2
GRID_W, HEAD_DIM, BLOCK, MIX_W, D_FF = 64, 64, 128, 512, 2816
HEADS_B, PAIRS_C, N_BRANCH = 4, 4, 3
ROPE_BASE, EPS, SCALE, NEG_INF = 10000.0, 1e-6, HEAD_DIM ** -0.5, -1e30
TOK = SEQ + CTX
NT = D_MODEL // P
KM = MIX_W // P
NF = D_FF // P
FH = NF // 2
NBLK, LBLK = TOK // P, SEQ // P
ADA_UNITS = 6 * NT
PRE_UNITS = 26
SLOT = FH * P

F32, F32R = mybir.dt.float32, mybir.dt.float32r
ALU, ACT = mybir.AluOpType, mybir.ActivationFunctionType
AX_X = mybir.AxisListType.X

LAT, CT, ALL = slice(0, SEQ), slice(SEQ, TOK), slice(0, TOK)
HALF_SWAP = [i ^ 16 for i in range(32)]

C_COS, C_SIN, C_ID, C_PREV, C_NEXT = 0, SEQ, 2 * SEQ, 2 * SEQ + P, 2 * SEQ + 2 * P
C_END = 2 * SEQ + 3 * P
V_ADA, V_N1, V_N2, V_SUB, V_CW, V_CB = 0, 48, 56, 64, 65, 65 + 3 * NF
V_END = V_CB + NF


class Count:

    def __init__(self):
        self.n, self.i, self.per = 0, None, 0

    def up(self, k=1):
        self.n += k
        return self.now()

    def begun(self):
        return self.i is not None or self.n > 0

    def now(self, back=0):
        return self.n - back if self.i is None else self.i * self.per + (self.n - back)


@contextmanager
def loop(eng, times, counts):
    start = {c: c.n for c in counts}
    with eng.Fori(0, times) as i:
        for c, per in counts.items():
            c.i, c.per = i, per
        yield i
    for c, per in counts.items():
        assert c.n - start[c] == per, (c.n - start[c], per)
        c.i, c.n = None, start[c] + per * times


def key_blocks(kind, b):
    if b >= LBLK:
        return [4, 5]
    if kind == "B":
        return list(range(NBLK))
    return [k for k in (b - 1, b, b + 1) if 0 <= k < LBLK] + [4, 5]


def key_runs(m, keys):
    runs, dst = [], m * TOK
    for k in keys:
        if runs and runs[-1][1] + runs[-1][2] == k * P and dst % 512:
            runs[-1][2] += P
        else:
            runs.append([dst, k * P, P])
        dst += P
    return runs


def unit_kinds():
    kinds = [("u", t) for t in range(KM)] + [("a", t) for t in range(KM)]
    for h in range(HEADS_B):
        kinds += [("q", h), ("k", h), ("v", h)]
    return kinds + [("ck", 0), ("cv", 0)] + [("cq", j) for j in range(PAIRS_C)]


KINDS = unit_kinds()
B_FIRST = 2 * KM
B_UNITS = range(B_FIRST, len(KINDS) - PAIRS_C + 1)
C_UNITS = range(B_UNITS.stop, len(KINDS))


def with_ctx(u, l):
    return l < DEPTH - 1 or KINDS[u][0] in ("k", "v", "ck", "cv")


def round_units(kind, h, b):
    if kind == "B" and b < 3:
        return [B_FIRST + 3 * (h + 1) + b]
    if kind == "C" and b == 0 and h + 1 < PAIRS_C:
        return [C_UNITS.start + h]
    return []


def blocks_of(l):
    return NBLK if l < DEPTH - 1 else LBLK


def attention_rounds(kind, l):
    return [(kind, h, b) for h in range(HEADS_B) for b in range(blocks_of(l))]


def tail_of(kind, h, b):
    return h - 1 if kind == "B" and b == 0 and h else None


def transpose_fills():
    fills = []
    for l in range(DEPTH):
        fills += [(l, "vn", t) for t in range(KM)] + [(l, "mix", g) for g in range(KM)] + [(l, "v", 0)]
        for kind in "BC":
            for _, h, b in attention_rounds(kind, l):
                fills.append((l, "p", kind, h, b, 0))
                if tail_of(kind, h, b) is not None:
                    fills.append((l, "oT", h - 1))
                if kind == "C":
                    fills.append((l, "p", kind, h, b, 1))
                fills.append((l, "o", kind, h, b))
                for u in round_units(kind, h, b):
                    if KINDS[u][0] in ("v", "cv"):
                        fills.append((l, "v", KINDS[u][1] if KINDS[u][0] == "v" else "c"))
            if kind == "B":
                fills.append((l, "oT", HEADS_B - 1))
    return {f: n + 1 for n, f in enumerate(fills)}


FILL = transpose_fills()
ROUND = {r: n + 1 for n, r in enumerate(
    (l, *r) for l in range(DEPTH) for kind in "BC" for r in attention_rounds(kind, l))}
SLOT_UNITS = (len(KINDS) + 2 * N_BRANCH * NT + NT + 2 * (2 * FH + NT)) // 2


def sums_before(l):
    return NT + 2 * NT * l


def width(l):
    return TOK if l < DEPTH - 1 else SEQ


def hybrid_prefix_dit_block(nc, t):
    ctx = ExitStack()
    with ctx:
        def sb(name, shape, dt=F32, scope=ctx):
            return scope.enter_context(nc.sbuf_tensor(name, shape, dt))

        def pb(name, shape):
            return ctx.enter_context(nc.psum_tensor(name, shape, F32))

        def sem(name):
            return ctx.enter_context(nc.semaphore(name))

        X = sb("X", [P, NT, TOK])
        Hhi, Hlo = sb("Hhi", [P, NT, TOK], F32R), sb("Hlo", [P, NT, TOK], F32R)
        raw = sb("raw", [P, 2, SLOT])
        Whi = [sb(f"Whi{s}", [P, SLOT], F32R) for s in range(2)]
        Wlo = [sb(f"Wlo{s}", [P, SLOT], F32R) for s in range(2)]
        consts, ones = sb("consts", [P, C_END]), sb("ones", [P, P])
        vecs = sb("vecs", [P, V_END])
        mod = sb("mod", [P, 6, NT, 2])
        gain = [sb(f"gain{i}", [P, NT, 2]) for i in range(2)]
        cond_in = sb("cond_in", [P, 2, NT])
        cond = sb("cond", [P, NT, 2])
        final_gain = sb("final_gain", [P, NT])
        lamv = sb("lamv", [P, 4, HEAD_DIM])
        lamp = sb("lamp", [P, 2, HEAD_DIM])
        small = sb("small", [P, 64])
        eps_col = sb("eps_col", [P, 1])
        sqacc = sb("sqacc", [P, TOK])
        tmp = sb("tmp", [P, 2, TOK])
        cos, sin = consts[:, C_COS:C_COS + SEQ], consts[:, C_SIN:C_SIN + SEQ]
        ident = consts[:, C_ID:C_ID + P]
        mask_prev, mask_next = consts[:, C_PREV:C_PREV + P], consts[:, C_NEXT:C_NEXT + P]

        with ExitStack() as mix:
            Y = sb("Y", [P, NT, TOK], F32, mix)
            Ohi, Olo = sb("Ohi", [P, KM, TOK], F32R, mix), sb("Olo", [P, KM, TOK], F32R, mix)
            with ExitStack() as gating:
                U = sb("U", [P, KM, TOK], F32, gating)
                VN = sb("VN", [P, NBLK, MIX_W], F32, gating)
                VF = sb("VF", [P, TOK], F32, gating)
                ln_rows = sb("ln_rows", [P, 2, MIX_W], F32, gating)
                wsT = sb("wsT", [P, KM, P], F32, gating)
                bs_rows = sb("bs_rows", [P, KM, P], F32, gating)
                bn = sb("bn", [P, NBLK, 6], F32, gating)
            Q = [sb(f"Q{i}", [P, TOK], F32, mix) for i in range(2)]
            K = [sb(f"K{i}", [P, TOK], F32, mix) for i in range(2)]
            V = [sb(f"V{i}", [P, NBLK, P], F32, mix) for i in range(2)]
            prob = [sb(f"prob{i}", [P, 2, TOK], F32, mix) for i in range(2)]
            AT = sb("AT", [P, NBLK, P], F32, mix)
            Oraw = sb("Oraw", [P, NBLK, P], F32, mix)
            stat = [sb(f"stat{i}", [P, 32], F32, mix) for i in range(2)]
            square = sb("square", [P, P], F32, mix)

        VT = sqacc

        with ExitStack() as ffn:
            Ghi, Glo = sb("Ghi", [P, FH, TOK], F32R, ffn), sb("Glo", [P, FH, TOK], F32R, ffn)
            apad = sb("apad", [P, TOK + 3], F32, ffn)
            conv, th = sb("conv", [P, TOK + 1], F32, ffn), sb("th", [P, TOK + 1], F32, ffn)
        diag = K[1]

        psL = pb("psL", [P, 2, 512])
        psC = pb("psC", [P, 512])
        psS = pb("psS", [P, 2 * TOK])
        psT = pb("psT", [P, 1024])
        PV = slice(TOK, TOK + P)
        RSTD = slice(512, 512 + TOK)
        maps = psS[:, :].rearrange("p (m c) -> p m c", m=2)

        loaded = [sem(f"loaded{s}") for s in range(2)]
        raw_read = [sem(f"raw_read{s}") for s in range(2)]
        consts_loaded, x_loaded, cond_loaded, vecs_loaded, gating_loaded, stored = (sem(n) for n in (
            "consts_loaded", "x_loaded", "cond_loaded", "vecs_loaded", "gating_loaded", "stored"))
        ones_ready, cond_ready, mod_ready, pads_ready, fin_ready = (sem(n) for n in (
            "ones_ready", "cond_ready", "mod_ready", "pads_ready", "fin_ready"))
        hi_ready = sem("hi_ready")
        lat_done, ctx_done = sem("lat_done"), sem("ctx_done")
        lat_read, ctx_read = [sem(f"lat_read{s}") for s in range(2)], sem("ctx_read")
        act_step, dve_step = sem("act_step"), sem("dve_step")
        sq_ready, acc_ready, sum_done, std_ready, diag_ready, rstd_done = (sem(n) for n in (
            "sq_ready", "acc_ready", "sum_done", "std_ready", "diag_ready", "rstd_done"))
        xn_ready, h_hi, h_ready = sem("xn_ready"), sem("h_hi"), sem("h_ready")
        t_done, t_read = sem("t_done"), sem("t_read")
        ln_var, ln_std, ln_ready = sem("ln_var"), sem("ln_std"), sem("ln_ready")
        mixed, mixed_hi, mixed_ready = sem("mixed"), sem("mixed_hi"), sem("mixed_ready")
        y_ready = sem("y_ready")
        qk_ready = sem("qk_ready")
        map0_done = sem("map0_done")
        scores_done, bias_ready, exp_done, prob_ready = (sem(n) for n in (
            "scores_done", "bias_ready", "exp_done", "prob_ready"))
        head_std, head_ready, o_hi = sem("head_std"), sem("head_ready"), sem("o_hi")
        conv_ready, th_ready, g_hi, g_ready = (sem(n) for n in ("conv_ready", "th_ready", "g_hi", "g_ready"))
        lam_dot, lam_exp = sem("lam_dot"), sem("lam_exp")

        LAMSUM, LAMEXP, NEGLAM, SUBG, NEGSINK, SINK, XSTD, XREC, LNMV, LNSTD = 0, 2, 4, 5, 8, 16, 24, 30, 36, 48
        MX, NB, SUM, REC, SINKB, SINKE, SSQ, HSTD = 0, 2, 4, 6, 8, 10, 12, 18

        block = ctx.enter_context(nc.Block())

        @block.sync
        def _(sp):
            n_load = [Count(), Count()]

            def load(slot, src, nk):
                if n_load[slot].begun():
                    sp.wait_ge(raw_read[slot], n_load[slot].now())
                sp.dma_start(raw[:, slot, 0:nk * P], src).then_inc(loaded[slot], 16)
                n_load[slot].up()

            def pairs(times, slot, first, second):
                with loop(sp, times, {n_load[0]: 1, n_load[1]: 1}) as i:
                    load(slot, *first(i))
                    load(1 - slot, *second(i))

            sp.dma_start(consts[:, :], t["consts"]).then_inc(consts_loaded, 16)
            sp.dma_start(final_gain[:, :], t["final_g"]).then_inc(consts_loaded, 16)
            sp.dma_start(cond_in[:, 0, :], t["c"]).then_inc(cond_loaded, 16)
            sp.dma_start(cond_in[:, 1, :], t["c_ctx"]).then_inc(cond_loaded, 16)
            for l in range(DEPTH):
                w_ada, w_in = t["w_ada"], t["w_in"]
                for s in range(2):
                    load(s, w_ada[l, s], NT)
                if l == 0:
                    sp.dma_start(X[:, :, LAT], t["x"]).then_inc(x_loaded, 16)
                    sp.dma_start(X[:, :, CT], t["ctx"]).then_inc(x_loaded, 16)
                else:
                    sp.wait_ge(acc_ready, sums_before(l))
                sp.dma_start(vecs[:, :], t["vecs"][l]).then_inc(vecs_loaded, 16)
                sp.dma_start(lamv[:, :, :], t["lam"][l].partition_broadcast(P)).then_inc(vecs_loaded, 16)
                sp.dma_start(small[:, SINK:SINK + 8], t["sinks"][l].partition_broadcast(P)).then_inc(vecs_loaded, 16)
                sp.dma_start(ln_rows[:, :, :], t["ln"][l].partition_broadcast(P)).then_inc(gating_loaded, 16)
                sp.dma_start(wsT[:, :, :], t["w_s"][l]).then_inc(gating_loaded, 16)
                sp.dma_start(bs_rows[:, :, :], t["b_s"][l].partition_broadcast(P)).then_inc(gating_loaded, 16)
                pairs(ADA_UNITS // 2 - 1, 0, lambda i: (w_ada[l, 2 * i + 2], NT), lambda i: (w_ada[l, 2 * i + 3], NT))

                def merge_units(i, slot):
                    pairs(NT, slot, lambda n: (w_in[l, n + (len(KINDS) + i * NT)], NT),
                          lambda n: (t["w_branch"][l, n + i * NT], KM))

                for u in range(B_FIRST):
                    load(u % 2, w_in[l, u], NT)
                merge_units(0, 0)
                for u in B_UNITS:
                    load(u % 2, w_in[l, u], NT)
                merge_units(1, B_UNITS.stop % 2)
                for u in C_UNITS:
                    load(u % 2, w_in[l, u], NT)
                merge_units(2, 0)
                pairs(NT // 2, 0, lambda i: (t["w_out"][l, 2 * i], NT), lambda i: (t["w_out"][l, 2 * i + 1], NT))
                for f in range(2):
                    pairs(FH, 0, lambda i: (t["w_gate"][l, i + f * FH], NT), lambda i: (t["w_up"][l, i + f * FH], NT))
                    pairs(NT // 2, 0, lambda i: (t["w_down"][l, 2 * i + f * NT], FH),
                          lambda i: (t["w_down"][l, 2 * i + (f * NT + 1)], FH))
            for n in range(NT):
                sp.wait_ge(fin_ready, n + 1)
                sp.dma_start(t["out"][:, n, :], X[:, n, LAT]).then_inc(stored, 16)
            sp.wait_ge(stored, 16 * NT)

        @block.gpsimd
        def _(pool):
            nc.gpsimd.memset(ones[:, :], 1.0).then_inc(ones_ready, 1)
            nc.gpsimd.memset(eps_col[:, :], EPS).then_inc(ones_ready, 1)
            for l in range(DEPTH):
                pool.wait_ge(acc_ready, sums_before(l) + NT)
                nc.gpsimd.memset(apad[:, 0:1], 0.0)
                nc.gpsimd.memset(apad[:, SEQ + 1:SEQ + 2], 0.0)
                nc.gpsimd.memset(apad[:, TOK + 2:TOK + 3], 0.0).then_inc(pads_ready, 1)

        @block.tensor
        def _(pe):
            n_unit, n_lat, n_ctx, n_load, n_h = Count(), [Count(), Count()], Count(), [Count(), Count()], Count()
            n_qk = Count()

            def unit(slot, nk, hi, lo, ctx_too, tiles_ready=None):
                pe.wait_ge(hi_ready, n_unit.up())
                pe.wait_ge(raw_read[slot], n_load[slot].up())
                if n_lat[slot].begun():
                    pe.wait_ge(lat_read[slot], n_lat[slot].now())
                n_lat[slot].up()
                for part in range(2 if ctx_too else 1):
                    cols = CT if part else LAT
                    out = psC[:, 0:CTX] if part else psL[:, slot, :]
                    if part and n_ctx.begun():
                        pe.wait_ge(ctx_read, n_ctx.now())
                    for k in range(nk):
                        if tiles_ready and not part:
                            pe.wait_ge(*tiles_ready(k))
                        w = slice(k * P, (k + 1) * P)
                        nc.tensor.matmul(out, Whi[slot][:, w], hi[:, k, cols], start=(k == 0), stop=False)
                        nc.tensor.matmul(out, Whi[slot][:, w], lo[:, k, cols], start=False, stop=False)
                        mm = nc.tensor.matmul(out, Wlo[slot][:, w], hi[:, k, cols], start=False, stop=(k == nk - 1))
                    mm.then_inc(ctx_done if part else lat_done, 1)
                if ctx_too:
                    n_ctx.up()

            def psT_free(fill):
                if FILL[fill] > 1:
                    pe.wait_ge(t_read, FILL[fill] - 1)

            def turn(fill, tiles):
                psT_free(fill)
                for k, src in enumerate(tiles):
                    mm = nc.tensor.transpose(psT[:, k * P:(k + 1) * P], src, ident)
                mm.then_inc(t_done, 1)

            def evacuated(slot, ctx_back=0):
                pe.wait_ge(lat_read[slot], n_lat[slot].now())
                pe.wait_ge(ctx_read, n_ctx.now(ctx_back))

            def norm_sums(ready, tok):
                pe.wait_ge(acc_ready, ready)
                for b in range(tok // P):
                    mm = nc.tensor.matmul(psS[:, b:b + 1], sqacc[:, b * P:(b + 1) * P], ones[:, 0:1],
                                          start=True, stop=True)
                mm.then_inc(sum_done, 1)
                n = (n_norm.up())
                pe.wait_ge(diag_ready, n)
                for c0, c1 in ((0, 512), (512, TOK)):
                    if c0 < tok:
                        mm = nc.tensor.matmul(psS[:, 512 + c0:512 + c1], ones[:, :], diag[:, c0:c1],
                                              start=True, stop=True)
                mm.then_inc(rstd_done, 1)

            n_norm = Count()

            def values(l, h):
                evacuated(slot_of_v[h])
                turn((l, "v", h), [VT[:, k * P:(k + 1) * P] for k in range(NBLK)])

            slot_of_v = {h: u % 2 for u, (kind, i) in enumerate(KINDS) if kind in ("v", "cv")
                         for h in ([i] if kind == "v" else ["c"])}

            def scores(l, kind, h, b):
                if ROUND[l, kind, h, b] > 1:
                    pe.wait_ge(exp_done, ROUND[l, kind, h, b] - 1)
                if b == 0:
                    pe.wait_ge(qk_ready, n_qk.up(2 if kind == "B" or h == 0 else 1))
                    pe.wait_ge(ctx_read, n_ctx.now())
                keys = K[h % 2] if kind == "B" else K[0]

                def products(m, runs):
                    rows = slice(m * HEAD_DIM, (m + 1) * HEAD_DIM)
                    for dst, src, n in runs:
                        mm = nc.tensor.matmul(psS[:, dst:dst + n], Q[h % 2][rows, b * P:(b + 1) * P],
                                              keys[rows, src:src + n], start=True, stop=True, skip_group_check=True)
                    return mm
                products(0, key_runs(0, key_blocks(kind, b))).then_inc(map0_done, 1)
                runs = key_runs(1, key_blocks(kind, b))
                if any(r[0] >= 1024 for r in runs):
                    products(1, [r for r in runs if r[0] >= 1024])
                pe.wait_ge(map0_done, ROUND[l, kind, h, b])
                products(1, [r for r in runs if r[0] < 1024]).then_inc(scores_done, 1)

            def attention_round(l, kind, h, b):
                keys = key_blocks(kind, b)
                pr = prob[ROUND[l, kind, h, b] % 2]
                pe.wait_ge(prob_ready, ROUND[l, kind, h, b])
                for m in range(1 if kind == "B" else 2):
                    turn((l, "p", kind, h, b, m), [pr[:, m, k * P:(k + 1) * P] for k in range(len(keys))])
                    if m == 0:
                        for u in round_units(kind, h, b):
                            unit(u % 2, NT, Hhi, Hlo, with_ctx(u, l))
                        if tail_of(kind, h, b) is not None:
                            head_out(l, h - 1)
                    fill = FILL[l, "p", kind, h, b, m]
                    pe.wait_ge(t_read, fill)
                    if kind == "B":
                        psT_free((l, "o", kind, h, b))
                        v = V[h % 2]
                    rows = slice(m * HEAD_DIM, (m + 1) * HEAD_DIM)
                    for k, kb in enumerate(keys):
                        flags = dict(start=(k == 0), stop=(k == len(keys) - 1))
                        if kind == "B":
                            mm = nc.tensor.matmul(psT[:, PV], AT[:, k, :], v[:, kb, :], **flags)
                        else:
                            mm = nc.tensor.matmul(psT[rows, PV], V[0][:, kb, rows], AT[:, k, :], **flags)
                mm.then_inc(t_done, 1)
                for u in round_units(kind, h, b):
                    if KINDS[u][0] in ("v", "cv"):
                        values(l, KINDS[u][1] if KINDS[u][0] == "v" else "c")

            def head_out(l, h):
                pe.wait_ge(head_ready, HEADS_B * l + h + 1)
                turn((l, "oT", h), [Oraw[:, k, :] for k in range(blocks_of(l))])

            def attention(l, kind):
                todo = attention_rounds(kind, l)
                scores(l, *todo[0])
                for n, r in enumerate(todo):
                    if n + 1 < len(todo):
                        scores(l, *todo[n + 1])
                    attention_round(l, *r)
                if kind == "B":
                    head_out(l, HEADS_B - 1)

            def merge(l, slot):
                c = l < DEPTH - 1
                with loop(pe, NT, {n_unit: 2, n_lat[0]: 1, n_lat[1]: 1, n_load[0]: 1, n_load[1]: 1, n_ctx: 2 * c}):
                    unit(slot, NT, Hhi, Hlo, c)
                    unit(1 - slot, KM, Ohi, Olo, c)

            pe.wait_ge(ones_ready, 2)
            pe.wait_ge(consts_loaded, 32)
            pe.wait_ge(cond_ready, 1)
            for l in range(DEPTH):
                c = l < DEPTH - 1
                blocks = blocks_of(l)
                per_pair = {n_unit: 2, n_lat[0]: 1, n_lat[1]: 1, n_load[0]: 1, n_load[1]: 1, n_ctx: 2 * c}
                with loop(pe, ADA_UNITS // 2, {n_load[0]: 1, n_load[1]: 1}) as i:
                    for s in range(2):
                        n_load[s].up()
                        pe.wait_ge(loaded[s], n_load[s].now() * 16)
                        for k in range(NT):
                            mm = nc.tensor.matmul(psS[:, bass.ds(i * 4 + 2 * s, 2)], raw[:, s, k * P:(k + 1) * P],
                                                  cond[:, k, :], start=(k == 0), stop=(k == NT - 1))
                        mm.then_inc(raw_read[s], 1)
                pe.wait_ge(mod_ready, l + 1)
                norm_sums(sums_before(l), TOK)
                for u in range(B_FIRST):
                    unit(u % 2, NT, Hhi, Hlo, c,
                         (lambda k: (h_ready, n_h.up())) if u == 0 else None)
                    if u > KM:
                        evacuated(1 - u % 2, 1 if c else 0)
                        turn((l, "vn", u - KM - 1), [VF[:, k * P:(k + 1) * P] for k in range(blocks)])
                evacuated(1)
                turn((l, "vn", KM - 1), [VF[:, k * P:(k + 1) * P] for k in range(blocks)])
                pe.wait_ge(ln_ready, l + 1)
                pe.wait_ge(gating_loaded, 48 * (l + 1))
                for g in range(KM):
                    psT_free((l, "mix", g))
                    for b in range(blocks):
                        mm = nc.tensor.matmul(psT[:, b * P:(b + 1) * P], VN[:, b, g * P:(g + 1) * P],
                                              wsT[:, g, :], start=True, stop=True, skip_group_check=True)
                    mm.then_inc(t_done, 1)
                pe.wait_ge(mixed_ready, KM * (l + 1))
                merge(l, 0)
                for u in B_UNITS[:3]:
                    unit(u % 2, NT, Hhi, Hlo, with_ctx(u, l))
                values(l, 0)
                attention(l, "B")
                pe.wait_ge(t_read, FILL[l, "oT", HEADS_B - 1])
                merge(l, B_UNITS.stop % 2)
                attention(l, "C")
                last = attention_rounds("C", l)[-1]
                pe.wait_ge(t_read, FILL[(l, "o", *last)])
                merge(l, 0)
                unit(0, NT, Hhi, Hlo, c, lambda k: (h_ready, n_h.up()))
                unit(1, NT, Hhi, Hlo, c)
                with loop(pe, NT // 2 - 1, per_pair):
                    unit(0, NT, Hhi, Hlo, c)
                    unit(1, NT, Hhi, Hlo, c)
                norm_sums(sums_before(l) + NT, width(l))
                for f in range(2):
                    unit(0, NT, Hhi, Hlo, c, (lambda k: (h_ready, n_h.up())) if f == 0 else None)
                    unit(1, NT, Hhi, Hlo, c)
                    with loop(pe, FH - 1, per_pair):
                        unit(0, NT, Hhi, Hlo, c)
                        unit(1, NT, Hhi, Hlo, c)
                    base = FH * (2 * l + f)
                    unit(0, FH, Ghi, Glo, c, lambda k: (g_ready, base + k + 1))
                    unit(1, FH, Ghi, Glo, c)
                    with loop(pe, NT // 2 - 1, per_pair):
                        unit(0, FH, Ghi, Glo, c)
                        unit(1, FH, Ghi, Glo, c)
            norm_sums(sums_before(DEPTH), SEQ)

        @block.scalar
        def _(act):
            n_lat, n_ctx, n_load, n_step = Count(), Count(), [Count(), Count()], Count()
            n_slot = [Count(), Count()]
            n_sq, n_norm, n_xn, n_conv = Count(), Count(), Count(), Count()

            def link(ins):
                ins.then_inc(act_step, 1)
                act.wait_ge(act_step, n_step.up())

            def split(slot, nk):
                act.wait_ge(loaded[slot], n_load[slot].up() * 16)
                if n_lat.begun():
                    act.wait_ge(lat_done, n_lat.now())
                if n_ctx.begun():
                    act.wait_ge(ctx_done, n_ctx.now())
                nc.scalar.activation(Whi[slot][:, 0:nk * P], raw[:, slot, 0:nk * P], ACT.Copy).then_inc(hi_ready, 1)

            def passed(slot, ctx_too):
                n_lat.up()
                n_slot[slot].up()
                if ctx_too:
                    n_ctx.up()

            def take(slot, ctx_too, lat_out, ctx_out, func, scale=1.0):
                passed(slot, ctx_too)
                act.wait_ge(lat_done, n_lat.now())
                nc.scalar.activation(lat_out, psL[:, slot, :], func, scale=scale).then_inc(lat_read[slot], 1)
                if ctx_too:
                    act.wait_ge(ctx_done, n_ctx.now())
                    nc.scalar.activation(ctx_out, psC[:, 0:CTX], func, scale=scale).then_inc(ctx_read, 1)

            def square_tile(n, slot, w):
                n_sq.up()
                if n_sq.i is not None or n_sq.n > 2:
                    act.wait_ge(acc_ready, n_sq.now(2))
                nc.scalar.activation(tmp[:, slot, 0:w], X[:, n, 0:w], ACT.Square).then_inc(sq_ready, 1)

            def updated(slot, ctx_too):
                act.wait_ge(lat_read[slot], n_slot[slot].now())
                if ctx_too:
                    act.wait_ge(ctx_read, n_ctx.now())

            def rms(tok):
                act.wait_ge(sum_done, n_norm.up())
                nc.scalar.activation(small[:, XSTD:XSTD + tok // P], psS[:, 0:tok // P], ACT.Sqrt,
                                     scale=1.0 / D_MODEL, bias=eps_col[:, :]).then_inc(std_ready, 1)

            def norm(tok, g, shift):
                rms(tok)
                for n in range(NT):
                    act.wait_ge(xn_ready, n_xn.up())
                    buf = tmp[:, n % 2, :]
                    ins = nc.scalar.activation(buf[:, LAT], buf[:, LAT], ACT.Identity,
                                               scale=gain[g][:, n, 0:1], bias=mod[:, shift, n, 0:1])
                    if tok > SEQ:
                        ins = nc.scalar.activation(buf[:, CT], buf[:, CT], ACT.Identity,
                                                   scale=gain[g][:, n, 1:2], bias=mod[:, shift, n, 1:2])
                    link(ins)
                    nc.scalar.activation(Hhi[:, n, 0:tok], buf[:, 0:tok], ACT.Copy).then_inc(h_hi, 1)

            def exps(l, kind, h, b):
                r = ROUND[l, kind, h, b]
                nk = len(key_blocks(kind, b)) * P
                st = stat[r % 2]
                act.wait_ge(bias_ready, r)
                if kind == "C":
                    nc.scalar.activation(st[:, SINKE:SINKE + 2], st[:, SINKB:SINKB + 2], ACT.Exp)
                for m in range(2):
                    ins = nc.scalar.activation(prob[r % 2][:, m, 0:nk], psS[:, m * TOK:m * TOK + nk], ACT.Exp,
                                               scale=SCALE, bias=st[:, NB + m:NB + m + 1],
                                               accum_out=st[:, SUM + m:SUM + m + 1])
                ins.then_inc(exp_done, 1)

            def copy_turned(l, kind, h, b, m):
                nk = len(key_blocks(kind, b))
                act.wait_ge(t_done, FILL[l, "p", kind, h, b, m])
                nc.scalar.activation(AT[:, 0:nk, :], psT[:, 0:nk * P].rearrange("p (k q) -> p k q", q=P),
                                     ACT.Copy).then_inc(t_read, 1)

            def head_out(l, h):
                w = width(l)
                act.wait_ge(t_done, FILL[l, "oT", h])
                nc.scalar.activation(Ohi[:, h, 0:w], psT[:, 0:w], ACT.Copy,
                                     scale=small[:, SUBG:SUBG + 1]).then_inc(o_hi, 1)

            def values(l, h):
                act.wait_ge(t_done, FILL[l, "v", h])
                nc.scalar.activation(V[0 if h == "c" else h % 2][:, :, :], psT[:, 0:TOK].rearrange(
                    "p (k q) -> p k q", q=P), ACT.Copy).then_inc(t_read, 1)

            def input_unit(l, u):
                split((u + 1) % 2, NT)
                if KINDS[u][0] in ("v", "cv"):
                    take(u % 2, with_ctx(u, l), VT[:, LAT], VT[:, CT], ACT.Copy)
                else:
                    passed(u % 2, with_ctx(u, l))

            def attention(l, kind):
                todo = attention_rounds(kind, l)
                nb = blocks_of(l)
                exps(l, *todo[0])
                for n, (_, h, b) in enumerate(todo):
                    copy_turned(l, kind, h, b, 0)
                    if n + 1 < len(todo):
                        exps(l, *todo[n + 1])
                    for u in round_units(kind, h, b):
                        input_unit(l, u)
                    if tail_of(kind, h, b) is not None:
                        head_out(l, h - 1)
                    if kind == "C":
                        copy_turned(l, kind, h, b, 1)
                    act.wait_ge(t_done, FILL[l, "o", kind, h, b])
                    if kind == "B":
                        nc.scalar.activation(square[:, :], psT[:, PV], ACT.Square,
                                             accum_out=stat[0][:, SSQ + b:SSQ + b + 1])
                        nc.scalar.activation(Oraw[:, b, :], psT[:, PV], ACT.Copy).then_inc(t_read, 1)
                        if b == nb - 1:
                            act.wait_ge(t_read, FILL[l, "o", kind, h, b])
                            nc.scalar.activation(stat[0][:, HSTD:HSTD + nb], stat[0][:, SSQ:SSQ + nb], ACT.Sqrt,
                                                 scale=1.0 / P, bias=eps_col[:, :]).then_inc(head_std, 1)
                    else:
                        nc.scalar.activation(Ohi[:, h, b * P:(b + 1) * P], psT[:, PV], ACT.Copy).then_inc(o_hi, 1)
                    for u in round_units(kind, h, b):
                        if KINDS[u][0] in ("v", "cv"):
                            values(l, KINDS[u][1] if KINDS[u][0] == "v" else "c")
                if kind == "B":
                    head_out(l, HEADS_B - 1)

            def merge(l, slot):
                c = l < DEPTH - 1
                with loop(act, NT, {n_lat: 2, n_ctx: 2 * c, n_load[0]: 1, n_load[1]: 1, n_slot[0]: 1, n_slot[1]: 1}):
                    split(1 - slot, KM)
                    updated(1 - slot, c)
                    take(slot, c, tmp[:, 0, LAT], tmp[:, 0, CT], ACT.Tanh, 0.5)
                    split(slot, NT)
                    passed(1 - slot, c)

            def x_tile(l, n, slot, next_nk, squares):
                c = l < DEPTH - 1
                if next_nk:
                    split(1 - slot, next_nk)
                passed(slot, c)
                if squares:
                    updated(slot, c)
                    square_tile(n, slot, width(l))

            def ffn_tile(l, f, i, next_nk):
                c = l < DEPTH - 1
                w = TOK + 1 if c else SEQ
                split(1, NT)
                if n_conv.begun():
                    act.wait_ge(conv_ready, n_conv.now())
                take(0, c, apad[:, 1:SEQ + 1], apad[:, SEQ + 2:TOK + 2], ACT.Copy)
                act.wait_ge(conv_ready, n_conv.up())
                nc.scalar.activation(th[:, 0:w], conv[:, 0:w], ACT.Tanh, scale=0.5).then_inc(th_ready, 1)
                split(0, next_nk)
                passed(1, c)
                updated(1, c)
                nc.scalar.activation(Ghi[:, i, 0:width(l)], tmp[:, 0, 0:width(l)], ACT.Copy).then_inc(g_hi, 1)

            act.wait_ge(cond_loaded, 32)
            nc.scalar.activation(cond[:, :, :].rearrange("p n m -> p m n"), cond_in[:, :, :], ACT.Silu).then_inc(cond_ready, 1)
            act.wait_ge(x_loaded, 32)
            act.wait_ge(ones_ready, 2)
            for n in range(NT):
                square_tile(n, n % 2, TOK)
            for l in range(DEPTH):
                c = l < DEPTH - 1
                per_pair = {n_lat: 2, n_ctx: 2 * c, n_load[0]: 1, n_load[1]: 1, n_slot[0]: 1, n_slot[1]: 1}
                act.wait_ge(lam_dot, l + 1)
                nc.scalar.activation(small[:, LAMEXP:LAMEXP + 2], small[:, LAMSUM:LAMSUM + 2], ACT.Exp).then_inc(lam_exp, 1)
                for s in range(2):
                    n_load[s].up(ADA_UNITS // 2)
                split(0, NT)
                norm(TOK, 0, 0)
                for u in range(B_FIRST):
                    split((u + 1) % 2, NT)
                    tile = u % KM
                    if u < KM:
                        take(u % 2, c, U[:, tile, LAT], U[:, tile, CT], ACT.Gelu_apprx_tanh)
                    else:
                        if tile:
                            act.wait_ge(t_done, FILL[l, "vn", tile - 1])
                        take(u % 2, c, VF[:, LAT], VF[:, CT], ACT.Gelu_apprx_tanh)
                act.wait_ge(ln_var, l + 1)
                nb = blocks_of(l)
                nc.scalar.activation(small[:, LNSTD:LNSTD + nb],
                                     small[:, LNMV:LNMV + 2 * nb].rearrange("p (b s) -> p b s", s=2)[:, :, 1],
                                     ACT.Sqrt, bias=eps_col[:, :]).then_inc(ln_std, 1)
                for g in range(KM):
                    act.wait_ge(mixed, KM * l + g + 1)
                    nc.scalar.activation(Ohi[:, g, 0:width(l)], tmp[:, g % 2, 0:width(l)],
                                         ACT.Copy).then_inc(mixed_hi, 1)
                merge(l, 0)
                for u in B_UNITS[:3]:
                    input_unit(l, u)
                values(l, 0)
                attention(l, "B")
                merge(l, B_UNITS.stop % 2)
                attention(l, "C")
                merge(l, 0)
                act.wait_ge(y_ready, 2 * NT * (l + 1))
                act.wait_ge(lat_done, n_lat.now())
                if c:
                    act.wait_ge(ctx_done, n_ctx.now())
                for n in range(NT):
                    nc.scalar.activation(Hhi[:, n, 0:width(l)], Y[:, n, 0:width(l)], ACT.Copy, scale=0.5).then_inc(h_hi, 1)
                with loop(act, NT // 2, per_pair | {n_sq: 2}) as i:
                    for s in range(2):
                        x_tile(l, 2 * i + s, s, NT, True)
                norm(width(l), 1, 3)
                for f in range(2):
                    with loop(act, FH - 1, per_pair | {n_conv: 1}) as i:
                        ffn_tile(l, f, i, NT)
                    ffn_tile(l, f, FH - 1, FH)
                    squares = f == 1
                    with loop(act, NT // 2 - 1, per_pair | {n_sq: 2 * squares}) as i:
                        for s in range(2):
                            x_tile(l, 2 * i + s, s, FH, squares)
                    x_tile(l, NT - 2, 0, FH, squares)
                    x_tile(l, NT - 1, 1, NT if f == 0 else None, squares)
            rms(SEQ)

        @block.vector
        def _(dve):
            n_hi, n_lat, n_ctx, n_step = Count(), Count(), Count(), Count()
            n_slot = [Count(), Count()]
            n_acc, n_norm, n_hhi, n_ohi, n_th, n_ghi, n_conv, n_qk = (Count() for _ in range(8))

            def link(ins):
                ins.then_inc(dve_step, 1)
                dve.wait_ge(dve_step, n_step.up())

            def split(slot, nk):
                dve.wait_ge(hi_ready, n_hi.up())
                nc.vector.tensor_tensor(Wlo[slot][:, 0:nk * P], raw[:, slot, 0:nk * P],
                                        Whi[slot][:, 0:nk * P].bitcast(F32), ALU.subtract).then_inc(raw_read[slot], 1)

            def passed(slot, ctx_too):
                n_lat.up()
                n_slot[slot].up()
                if ctx_too:
                    n_ctx.up()

            def lo_part(out, full, hi):
                return nc.vector.tensor_tensor(out, full, hi.bitcast(F32), ALU.subtract)

            def add_square(slot, w):
                dve.wait_ge(sq_ready, n_acc.up())
                nc.vector.tensor_tensor(sqacc[:, 0:w], sqacc[:, 0:w], tmp[:, slot, 0:w], ALU.add).then_inc(acc_ready, 1)
                dve.wait_ge(acc_ready, n_acc.now())

            def rms(tok):
                dve.wait_ge(std_ready, n_norm.up())
                nb = tok // P
                link(nc.vector.reciprocal(small[:, XREC:XREC + nb], small[:, XSTD:XSTD + nb]))
                for b in range(nb):
                    ins = nc.vector.tensor_scalar(diag[:, b * P:(b + 1) * P], ident, small[:, XREC + b:XREC + b + 1],
                                                  None, ALU.mult)
                ins.then_inc(diag_ready, 1)
                dve.wait_ge(rstd_done, n_norm.now())

            def norm(tok):
                rms(tok)

                def finish(n):
                    dve.wait_ge(h_hi, n_hhi.up())
                    lo_part(Hlo[:, n, 0:tok], tmp[:, n % 2, 0:tok], Hhi[:, n, 0:tok]).then_inc(h_ready, 1)

                for n in range(NT):
                    if n > 1:
                        dve.wait_ge(h_ready, n_hhi.now())
                    nc.vector.tensor_tensor(tmp[:, n % 2, 0:tok], X[:, n, 0:tok], psS[:, RSTD][:, 0:tok],
                                            ALU.mult).then_inc(xn_ready, 1)
                    if n:
                        finish(n - 1)
                finish(NT - 1)

            def rotary(l, u, out):
                slot, ctx_too = u % 2, with_ctx(u, l)
                dve.wait_ge(lat_read[1 - slot], n_slot[1 - slot].now())
                dve.wait_ge(ctx_read, n_ctx.now())
                if n_qk.begun():
                    dve.wait_ge(qk_ready, n_qk.now())
                n_qk.up()
                passed(slot, ctx_too)
                dve.wait_ge(lat_done, n_lat.now())
                swapped, turned = tmp[:, 0, LAT], tmp[:, 1, LAT]
                link(nc.vector.stream_shuffle(swapped, psL[:, slot, :], HALF_SWAP))
                nc.vector.tensor_tensor(turned, psL[:, slot, :], cos, ALU.mult).then_inc(lat_read[slot], 1)
                link(nc.vector.tensor_tensor(swapped, swapped, sin, ALU.mult))
                nc.vector.tensor_tensor(out[:, LAT], turned, swapped, ALU.add).then_inc(qk_ready, 1)
                if ctx_too:
                    dve.wait_ge(ctx_done, n_ctx.now())
                    nc.vector.tensor_copy(out[:, CT], psC[:, 0:CTX]).then_inc(ctx_read, 1)

            def input_unit(l, u):
                split((u + 1) % 2, KM if False else NT)
                kind, h = KINDS[u]
                if kind in ("v", "cv"):
                    passed(u % 2, with_ctx(u, l))
                else:
                    rotary(l, u, {"q": Q, "k": K, "ck": K, "cq": Q}[kind][h % 2])

            def row_max(l, kind, h, b):
                r = ROUND[l, kind, h, b]
                st = stat[r % 2]
                keys = key_blocks(kind, b)
                dve.wait_ge(scores_done, r)
                if kind == "C" and b < LBLK:
                    for k, kb in enumerate(keys[:-2]):
                        if kb != b:
                            area = maps[:, :, k * P:(k + 1) * P]
                            mask = (mask_prev if kb < b else mask_next).unsqueeze(1).broadcast_to([P, 2, P])
                            link(nc.vector.tensor_tensor(area, area, mask, ALU.add))
                link(nc.vector.reduce_max(st[:, MX:MX + 2], maps[:, :, 0:len(keys) * P], AX_X))
                if kind == "B":
                    nc.vector.tensor_scalar(st[:, NB:NB + 2], st[:, MX:MX + 2], -SCALE, None, ALU.mult).then_inc(bias_ready, 1)
                else:
                    link(nc.vector.scalar_tensor_tensor(st[:, NB:NB + 2], st[:, MX:MX + 2], -SCALE,
                                                        small[:, NEGSINK + 2 * h:NEGSINK + 2 * h + 2], ALU.mult, ALU.min))
                    nc.vector.tensor_tensor(st[:, SINKB:SINKB + 2], st[:, NB:NB + 2],
                                            small[:, NEGSINK + 2 * h:NEGSINK + 2 * h + 2],
                                            ALU.subtract).then_inc(bias_ready, 1)

            def normalise(l, kind, h, b):
                r = ROUND[l, kind, h, b]
                st, pr = stat[r % 2], prob[r % 2]
                n = len(key_blocks(kind, b)) * P
                dve.wait_ge(exp_done, r)
                if kind == "C":
                    link(nc.vector.tensor_tensor(st[:, SUM:SUM + 2], st[:, SUM:SUM + 2], st[:, SINKE:SINKE + 2], ALU.add))
                link(nc.vector.reciprocal(st[:, REC:REC + 2], st[:, SUM:SUM + 2]))
                if kind == "B":
                    nc.vector.tensor_tensor(st[:, REC + 1:REC + 2], st[:, REC + 1:REC + 2],
                                            small[:, NEGLAM:NEGLAM + 1], ALU.mult)
                    link(nc.vector.tensor_scalar(pr[:, 0, 0:n], pr[:, 0, 0:n], st[:, REC:REC + 1], None, ALU.mult))
                    nc.vector.scalar_tensor_tensor(pr[:, 0, 0:n], pr[:, 1, 0:n], st[:, REC + 1:REC + 2],
                                                   pr[:, 0, 0:n], ALU.mult, ALU.add).then_inc(prob_ready, 1)
                else:
                    for m in range(2):
                        ins = nc.vector.tensor_scalar(pr[:, m, 0:n], pr[:, m, 0:n], st[:, REC + m:REC + m + 1],
                                                      None, ALU.mult)
                    ins.then_inc(prob_ready, 1)

            def head_out(l, h):
                w = width(l)
                dve.wait_ge(o_hi, n_ohi.up())
                nc.vector.scalar_tensor_tensor(Olo[:, h, 0:w], psT[:, 0:w], small[:, SUBG:SUBG + 1],
                                               Ohi[:, h, 0:w].bitcast(F32), ALU.mult, ALU.subtract).then_inc(t_read, 1)

            def attention(l, kind):
                todo = attention_rounds(kind, l)
                nb = blocks_of(l)
                row_max(l, *todo[0])
                for n, (_, h, b) in enumerate(todo):
                    normalise(l, kind, h, b)
                    if n + 1 < len(todo):
                        row_max(l, *todo[n + 1])
                    for u in round_units(kind, h, b):
                        input_unit(l, u)
                    if tail_of(kind, h, b) is not None:
                        head_out(l, h - 1)
                    if kind == "C":
                        dve.wait_ge(o_hi, n_ohi.up())
                        q = slice(b * P, (b + 1) * P)
                        lo_part(Olo[:, h, q], psT[:, PV], Ohi[:, h, q]).then_inc(t_read, 1)
                    elif b == nb - 1:
                        dve.wait_ge(head_std, HEADS_B * l + h + 1)
                        link(nc.vector.reciprocal(stat[0][:, HSTD:HSTD + nb], stat[0][:, HSTD:HSTD + nb]))
                        nc.vector.tensor_tensor(Oraw[:, 0:nb, :], Oraw[:, 0:nb, :],
                                                stat[0][:, HSTD:HSTD + nb].unsqueeze(2).broadcast_to([P, nb, P]),
                                                ALU.mult).then_inc(head_ready, 1)
                if kind == "B":
                    head_out(l, HEADS_B - 1)

            def merge(l, i, slot):
                c = l < DEPTH - 1
                w = width(l)
                with loop(dve, NT, {n_hi: 2, n_lat: 2, n_ctx: 2 * c, n_slot[0]: 1, n_slot[1]: 1}) as n:
                    split(1 - slot, KM)
                    passed(slot, c)
                    split(slot, NT)
                    passed(1 - slot, c)
                    out = Y[:, n, :] if i == 0 else tmp[:, 1, :]
                    dve.wait_ge(lat_done, n_lat.now())
                    dve.wait_ge(lat_read[slot], n_slot[slot].now())
                    nc.vector.scalar_tensor_tensor(out[:, LAT], tmp[:, 0, LAT], 1.0, psL[:, 1 - slot, :],
                                                   ALU.add, ALU.mult).then_inc(lat_read[1 - slot], 1)
                    if c:
                        dve.wait_ge(ctx_done, n_ctx.now())
                        dve.wait_ge(ctx_read, n_ctx.now(1))
                        nc.vector.scalar_tensor_tensor(out[:, CT], tmp[:, 0, CT], 1.0, psC[:, 0:CTX],
                                                       ALU.add, ALU.mult).then_inc(ctx_read, 1)
                    if i:
                        dve.wait_ge(lat_read[1 - slot], n_slot[1 - slot].now())
                        if c:
                            dve.wait_ge(ctx_read, n_ctx.now())
                        nc.vector.tensor_tensor(Y[:, n, 0:w], Y[:, n, 0:w], tmp[:, 1, 0:w],
                                                ALU.add).then_inc(y_ready, 1)

            def x_tile(l, n, slot, gate, next_nk, squares):
                c = l < DEPTH - 1
                if next_nk:
                    split(1 - slot, next_nk)
                passed(slot, c)
                dve.wait_ge(lat_done, n_lat.now())
                nc.vector.scalar_tensor_tensor(X[:, n, LAT], psL[:, slot, :], mod[:, gate, n, 0:1], X[:, n, LAT],
                                               ALU.mult, ALU.add).then_inc(lat_read[slot], 1)
                if c:
                    dve.wait_ge(ctx_done, n_ctx.now())
                    nc.vector.scalar_tensor_tensor(X[:, n, CT], psC[:, 0:CTX], mod[:, gate, n, 1:2], X[:, n, CT],
                                                   ALU.mult, ALU.add).then_inc(ctx_read, 1)
                if squares:
                    add_square(slot, width(l))

            def ffn_tile(l, f, i, next_nk):
                c = l < DEPTH - 1
                w = TOK + 1 if c else SEQ
                split(1, NT)
                passed(0, c)
                dve.wait_ge(lat_read[0], n_slot[0].now())
                if c:
                    dve.wait_ge(ctx_read, n_ctx.now())

                def tap(k):
                    return vecs[:, bass.ds(i + (V_CW + k * NF + f * FH), 1)]
                link(nc.vector.tensor_scalar(conv[:, 0:w], apad[:, 1:w + 1], tap(1), tap(3), ALU.mult, ALU.add))
                link(nc.vector.scalar_tensor_tensor(conv[:, 0:w], apad[:, 0:w], tap(0), conv[:, 0:w], ALU.mult, ALU.add))
                nc.vector.scalar_tensor_tensor(conv[:, 0:w], apad[:, 2:w + 2], tap(2), conv[:, 0:w],
                                               ALU.mult, ALU.add).then_inc(conv_ready, 1)
                dve.wait_ge(th_ready, n_th.up())
                link(nc.vector.scalar_tensor_tensor(conv[:, 0:w], th[:, 0:w], 1.0, conv[:, 0:w], ALU.add, ALU.mult))
                split(0, next_nk)
                passed(1, c)
                dve.wait_ge(lat_done, n_lat.now())
                nc.vector.scalar_tensor_tensor(tmp[:, 0, LAT], conv[:, 0:SEQ], 0.5, psL[:, 1, :],
                                               ALU.mult, ALU.mult).then_inc(lat_read[1], 1)
                if c:
                    dve.wait_ge(ctx_done, n_ctx.now())
                    nc.vector.scalar_tensor_tensor(tmp[:, 0, CT], conv[:, SEQ + 1:TOK + 1], 0.5, psC[:, 0:CTX],
                                                   ALU.mult, ALU.mult).then_inc(ctx_read, 1)
                dve.wait_ge(g_hi, n_ghi.up())
                wd = width(l)
                lo_part(Glo[:, i, 0:wd], tmp[:, 0, 0:wd], Ghi[:, i, 0:wd]).then_inc(g_ready, 1)

            link(nc.vector.memset(sqacc[:, :], 0.0))
            for n in range(NT):
                add_square(n % 2, TOK)
            for l in range(DEPTH):
                c = l < DEPTH - 1
                nb, w = blocks_of(l), width(l)
                lam_init = 0.8 - 0.6 * float(np.exp(-0.3 * l))
                dve.wait_ge(vecs_loaded, 48 * (l + 1))
                link(nc.vector.tensor_tensor(lamp[:, :, :], lamv[:, 0::2, :], lamv[:, 1::2, :], ALU.mult))
                nc.vector.reduce_sum(small[:, LAMSUM:LAMSUM + 2], lamp[:, :, :], AX_X).then_inc(lam_dot, 1)
                dve.wait_ge(lam_exp, l + 1)
                link(nc.vector.tensor_tensor(small[:, NEGLAM:NEGLAM + 1], small[:, LAMEXP + 1:LAMEXP + 2],
                                             small[:, LAMEXP:LAMEXP + 1], ALU.subtract))
                nc.vector.tensor_scalar(small[:, NEGLAM:NEGLAM + 1], small[:, NEGLAM:NEGLAM + 1], -lam_init, None, ALU.add)
                nc.vector.tensor_scalar(small[:, SUBG:SUBG + 1], vecs[:, V_SUB:V_SUB + 1], 1.0 - lam_init, None, ALU.mult)
                link(nc.vector.tensor_scalar(small[:, NEGSINK:NEGSINK + 8], small[:, SINK:SINK + 8], -1.0, None, ALU.mult))
                for s in range(2):
                    dve.wait_ge(raw_read[s], (ADA_UNITS // 2) * (l + 1) + SLOT_UNITS * l)
                link(nc.vector.tensor_tensor(
                    mod[:, :, :, :].rearrange("p c t m -> p (c t) m"),
                    psS[:, 0:2 * ADA_UNITS].rearrange("p (u m) -> p u m", m=2),
                    vecs[:, V_ADA:V_ADA + ADA_UNITS].unsqueeze(2).broadcast_to([P, ADA_UNITS, 2]), ALU.add))
                for g, col in ((0, V_N1), (1, V_N2)):
                    for m in range(2):
                        ins = nc.vector.scalar_tensor_tensor(gain[g][:, :, m], mod[:, 3 * g + 1, :, m], 1.0,
                                                             vecs[:, col:col + NT], ALU.add, ALU.mult)
                ins.then_inc(mod_ready, 1)
                split(0, NT)
                norm(TOK)
                for u in range(B_FIRST + 1):
                    if u < B_FIRST:
                        split((u + 1) % 2, NT)
                        passed(u % 2, c)
                    if u > KM:
                        tile = u - KM - 1
                        dve.wait_ge(t_done, FILL[l, "vn", tile])
                        nc.vector.tensor_copy(VN[:, 0:nb, tile * P:(tile + 1) * P],
                                              psT[:, 0:nb * P].rearrange("p (b q) -> p b q", q=P)).then_inc(t_read, 1)
                dve.wait_ge(t_read, FILL[l, "vn", KM - 1])
                for b in range(nb):
                    ins = nc.vector.bn_stats(bn[:, b, :], VN[:, b, :])
                link(ins)
                for b in range(nb):
                    ins = nc.vector.bn_aggr(small[:, LNMV + 2 * b:LNMV + 2 * b + 2], bn[:, b, :])
                ins.then_inc(ln_var, 1)
                dve.wait_ge(ln_std, l + 1)
                link(nc.vector.reciprocal(small[:, LNSTD:LNSTD + nb], small[:, LNSTD:LNSTD + nb]))
                for b in range(nb):
                    ins = nc.vector.tensor_scalar(VN[:, b, :], VN[:, b, :], small[:, LNMV + 2 * b:LNMV + 2 * b + 1],
                                                  small[:, LNSTD + b:LNSTD + b + 1], ALU.subtract, ALU.mult)
                link(ins)
                dve.wait_ge(gating_loaded, 48 * (l + 1))
                link(nc.vector.tensor_tensor(VN[:, 0:nb, :], VN[:, 0:nb, :],
                                             ln_rows[:, 0:1, :].broadcast_to([P, nb, MIX_W]), ALU.mult))
                nc.vector.tensor_tensor(VN[:, 0:nb, :], VN[:, 0:nb, :],
                                        ln_rows[:, 1:2, :].broadcast_to([P, nb, MIX_W]), ALU.add).then_inc(ln_ready, 1)
                for g in range(KM):
                    fill = FILL[l, "mix", g]
                    buf = tmp[:, g % 2, 0:w]
                    dve.wait_ge(t_done, fill)
                    nc.vector.tensor_tensor(buf.rearrange("p (b q) -> p b q", q=P),
                                            psT[:, 0:w].rearrange("p (b q) -> p b q", q=P),
                                            bs_rows[:, g:g + 1, :].broadcast_to([P, nb, P]), ALU.add).then_inc(t_read, 1)
                    dve.wait_ge(t_read, fill)
                    nc.vector.tensor_tensor(buf, buf, U[:, g, 0:w], ALU.mult).then_inc(mixed, 1)
                    dve.wait_ge(mixed_hi, KM * l + g + 1)
                    lo_part(Olo[:, g, 0:w], buf, Ohi[:, g, 0:w]).then_inc(mixed_ready, 1)
                merge(l, 0, 0)
                for u in B_UNITS[:3]:
                    input_unit(l, u)
                attention(l, "B")
                merge(l, 1, B_UNITS.stop % 2)
                attention(l, "C")
                merge(l, 2, 0)
                for n in range(NT):
                    dve.wait_ge(h_hi, n_hhi.up())
                    nc.vector.scalar_tensor_tensor(Hlo[:, n, 0:w], Y[:, n, 0:w], 0.5, Hhi[:, n, 0:w].bitcast(F32),
                                                   ALU.mult, ALU.subtract).then_inc(h_ready, 1)
                link(nc.vector.memset(sqacc[:, :], 0.0))
                per_pair = {n_hi: 2, n_lat: 2, n_ctx: 2 * c, n_slot[0]: 1, n_slot[1]: 1}
                with loop(dve, NT // 2, per_pair | {n_acc: 2}) as i:
                    for s in range(2):
                        x_tile(l, 2 * i + s, s, 2, NT, True)
                norm(w)
                link(nc.vector.memset(sqacc[:, :], 0.0))
                dve.wait_ge(pads_ready, l + 1)
                for f in range(2):
                    with loop(dve, FH - 1, per_pair | {n_th: 1, n_ghi: 1, n_step: 3}) as i:
                        ffn_tile(l, f, i, NT)
                    ffn_tile(l, f, FH - 1, FH)
                    squares = f == 1
                    with loop(dve, NT // 2 - 1, per_pair | {n_acc: 2 * squares}) as i:
                        for s in range(2):
                            x_tile(l, 2 * i + s, s, 5, FH, squares)
                    x_tile(l, NT - 2, 0, 5, FH, squares)
                    x_tile(l, NT - 1, 1, 5, NT if f == 0 else None, squares)
            rms(SEQ)
            for n in range(NT):
                nc.vector.scalar_tensor_tensor(X[:, n, LAT], X[:, n, LAT], final_gain[:, n:n + 1],
                                               psS[:, RSTD][:, LAT], ALU.mult, ALU.mult).then_inc(fin_ready, 1)


def constant_table():
    table = np.zeros((P, C_END), np.float32)
    half = HEAD_DIM // 2
    inv = (np.float32(ROPE_BASE) ** (-np.arange(0, half, 2, dtype=np.float32) / np.float32(half))).astype(np.float32)
    place = np.arange(SEQ)
    for p in range(P):
        axis = place // GRID_W if (p % HEAD_DIM) < half else place % GRID_W
        angle = axis.astype(np.float32) * inv[p % 16]
        table[p, C_COS:C_COS + SEQ] = np.cos(angle)
        table[p, C_SIN:C_SIN + SEQ] = np.sin(angle) * (-1 if p % 32 < 16 else 1)
    table[:, C_ID:C_ID + P] = np.eye(P)
    q, k = np.arange(P)[:, None], np.arange(P)[None, :]
    table[:, C_PREV:C_PREV + P] = np.where(k >= q, 0, NEG_INF)
    table[:, C_NEXT:C_NEXT + P] = np.where(k <= q, 0, NEG_INF)
    return table


def input_columns():
    start = {"u": 0, "a": MIX_W, "q": 2 * MIX_W, "k": 3 * MIX_W, "v": 4 * MIX_W, "ck": 6 * MIX_W, "cv": 6 * MIX_W + P}
    cols = []
    for kind, i in KINDS:
        if kind == "cq":
            cols += [np.arange(HEAD_DIM) + 5 * MIX_W + (g * PAIRS_C + i) * HEAD_DIM for g in range(2)]
        else:
            cols.append(np.arange(P) + start[kind] + i * P)
    return np.concatenate(cols + [np.arange(N_BRANCH * D_MODEL) + 6 * MIX_W + 2 * P])


def units(w):
    d, k, n = w.shape
    return np.ascontiguousarray(w.reshape(d, k // P, P, n // P, P).transpose(0, 3, 2, 1, 4)).reshape(d, n // P, P, k)


def per_feature(v):
    return np.ascontiguousarray(np.swapaxes(v.reshape(*v.shape[:-1], -1, P), -1, -2))


def laid_out(i):
    i = {k: np.asarray(v) for k, v in i.items()}
    rows = np.arange(MIX_W).reshape(2, PAIRS_C, HEAD_DIM).transpose(1, 0, 2).reshape(-1)
    branch = np.stack([i["w_branch"][:, 0], i["w_branch"][:, 1], i["w_branch"][:, 2][:, rows]], 1)
    half = D_FF // 2
    cw = i["conv_w"]
    return {
        "x": per_feature(i["x"][0]).transpose(1, 2, 0), "ctx": per_feature(i["ctx"][0]).transpose(1, 2, 0),
        "c": per_feature(i["c"][0]), "c_ctx": per_feature(i["c_ctx"]),
        "w_ada": units(i["w_ada"]), "w_in": units(i["w_in"][:, :, input_columns()]),
        "w_branch": np.concatenate([units(branch[:, n]) for n in range(N_BRANCH)], 1),
        "w_out": units(i["w_out"]), "w_gate": units(i["w_gate"]), "w_up": units(i["w_up"]),
        "w_down": np.concatenate([units(i["w_down"][:, f * half:(f + 1) * half]) for f in range(2)], 1),
        "vecs": np.concatenate([per_feature(v) for v in (
            i["b_ada"], i["norm1_g"], i["norm2_g"], i["diff_subln_g"], cw[:, 0], cw[:, 1], cw[:, 2], i["conv_b"])], -1),
        "lam": np.stack([i[n] for n in ("lam_q1", "lam_k1", "lam_q2", "lam_k2")], 1),
        "sinks": i["sinks"].reshape(DEPTH, 2, PAIRS_C).transpose(0, 2, 1).reshape(DEPTH, -1),
        "ln": np.stack([i["sgu_ln_g"], i["sgu_ln_b"]], 1),
        "w_s": i["w_s"].transpose(0, 3, 1, 2), "b_s": i["b_s"], "final_g": per_feature(i["final_g"]),
        "consts": constant_table(),
    }


def kernel(**inputs):
    import concourse.bacc as bacc
    from concourse.bass_utils import run_bass_kernel_spmd

    nc = bacc.Bacc("TRN2", target_bir_lowering=False, num_devices=1)
    arrays, tensors = {}, {}
    for name, a in laid_out(inputs).items():
        arrays[f"in_{name}"] = np.ascontiguousarray(a)
        tensors[name] = nc.dram_tensor(f"in_{name}", a.shape, mybir.dt.from_np(a.dtype), kind="ExternalInput").ap()
    tensors["out"] = nc.dram_tensor("out", (P, NT, SEQ), F32, kind="ExternalOutput").ap()
    hybrid_prefix_dit_block(nc, tensors)
    result = run_bass_kernel_spmd(nc, [arrays], core_ids=[0]).results[0]["out"]
    return np.ascontiguousarray(result.transpose(2, 1, 0)).reshape(1, SEQ, D_MODEL)
```

```python
from contextlib import ExitStack, contextmanager

import numpy as np

import concourse.bass as bass
from concourse import mybir

P = 128
D_MODEL, SEQ, CTX, DEPTH = 1024, 512, 256, 2
GRID_W, HEAD_DIM, MIX_W, D_FF = 64, 64, 512, 2816
HEADS_B, PAIRS_C, N_BRANCH = 4, 4, 3
ROPE_BASE, EPS, SCALE, NEG_INF = 10000.0, 1e-6, HEAD_DIM ** -0.5, -1e30
TOK = SEQ + CTX
NT = D_MODEL // P
KM = MIX_W // P
NF = D_FF // P
PARTS = ((0, 8), (8, 7), (15, 7))
NBLK, LBLK = TOK // P, SEQ // P
SLOT = NT * P
ADA_UNITS = 6 * NT
ADA_PE = 9
ADA_START = 3 * NT + 4
ADA_GROUP = 3

F32, F32R = mybir.dt.float32, mybir.dt.float32r
ALU, ACT = mybir.AluOpType, mybir.ActivationFunctionType
AX_X = mybir.AxisListType.X

LAT, CT = slice(0, SEQ), slice(SEQ, TOK)
HALF_SWAP = [i ^ 16 for i in range(32)]

C_COS, C_SIN, C_ID, C_PREV, C_NEXT = 0, SEQ, 2 * SEQ, 2 * SEQ + P, 2 * SEQ + 2 * P
C_END = 2 * SEQ + 3 * P
V_ADA, V_N1, V_N2, V_SUB, V_CW, V_CB = 0, 48, 56, 64, 65, 65 + 3 * NF
V_LNG, V_LNB = V_CB + NF, V_CB + NF + KM
V_END = V_LNB + KM


class Count:

    def __init__(self):
        self.n, self.i, self.per = 0, None, 0

    def up(self, k=1):
        self.n += k
        return self.now()

    def begun(self):
        return self.i is not None or self.n > 0

    def now(self, back=0):
        return self.n - back if self.i is None else self.i * self.per + (self.n - back)


@contextmanager
def loop(eng, times, counts):
    start = {c: c.n for c in counts}
    with eng.Fori(0, times) as i:
        for c, per in counts.items():
            c.i, c.per = i, per
        yield i
    for c, per in counts.items():
        assert c.n - start[c] == per, (c.n - start[c], per)
        c.i, c.n = None, start[c] + per * times


def key_blocks(kind, b):
    if b >= LBLK:
        return [4, 5]
    if kind == "B":
        return list(range(NBLK))
    return [k for k in (b - 1, b, b + 1) if 0 <= k < LBLK] + [4, 5]


def key_runs(m, keys):
    runs, dst = [], m * TOK
    for k in keys:
        if runs and runs[-1][1] + runs[-1][2] == k * P and dst % 512:
            runs[-1][2] += P
        else:
            runs.append([dst, k * P, P])
        dst += P
    return runs


def input_kinds():
    kinds = [("u", t) for t in range(KM)] + [("a", t) for t in range(KM)]
    for h in range(HEADS_B):
        kinds += [("q", h), ("k", h), ("v", h)]
    return kinds + [("ck", 0), ("cv", 0)] + [("cq", j) for j in range(PAIRS_C)]


KINDS = input_kinds()


def with_ctx(u, l):
    return l < DEPTH - 1 or u[0] in ("k", "v", "ck", "cv")


def tiles_of(u):
    return KM if u[0] == "branch" else NT


def blocks_of(l):
    return NBLK if l < DEPTH - 1 else LBLK


def mixer_steps(l):
    nb = blocks_of(l)
    steps = []
    made_qk = []

    def half(what, u, between=()):
        steps.append((what, u))
        steps.extend(between)
        if what == "half" and made_qk:
            steps.append(("split_qk", made_qk.pop()))
        if what == "unit" and u[0] in ("q", "k", "ck", "cq"):
            made_qk.append(u)

    def unit(*u, between=()):
        half("half", u, between)
        half("unit", u)

    def attention(kind, first, fillers):
        rounds = [(kind, h, b) for h in range(HEADS_B) for b in range(nb)]
        steps.extend([("scores", rounds[0]), ("exp", rounds[0])])
        unit(*first, between=[("norm", rounds[0])])
        waiting = None
        for n, r in enumerate(rounds):
            after = rounds[n + 1] if n + 1 < len(rounds) else None
            if after:
                steps.append(("scores", after))
            steps.append(("turn", r, 0))
            between = []
            if after:
                steps.extend([("exp", after), ("norm", after)])
            if kind == "C":
                between.append(("turn", r, 1))
            halves = [(what, u) for u in fillers[r[1]] for what in ("half", "unit")]
            for j, (what, u) in enumerate(halves):
                if j * nb // len(halves) != r[2]:
                    continue
                half(what, u, between)
                between = []
                if what == "half" and waiting is not None:
                    steps.append(("values", waiting))
                    waiting = None
                if what == "unit" and u[0] == "v":
                    waiting = u[1]
            steps.extend(between + [("out", r)])

    def merge(i, n):
        return [("gate", i, n), ("branch", i, n)]

    for k in range(KM):
        unit("a", k)
        if k:
            steps.append(("vn", k - 1))
    unit("u", 0)
    steps.extend([("vn", KM - 1), ("ln",)])
    for k in range(1, KM):
        unit("u", k)
        if k == 1:
            steps.append(("rowsum",))
    for g, u in enumerate((("q", 0), ("k", 0), ("v", 0), ("gate", 0, 0))):
        steps.append(("mix", g))
        unit(*u)
    steps.append(("values", 0))
    unit("branch", 0, 0)
    heads = [[("q", h), ("k", h), ("v", h)] for h in range(1, HEADS_B)]
    attention("B", ("gate", 0, 1), [
        [("branch", 0, 1)] + heads[0] + merge(0, 2),
        heads[1] + merge(0, 3) + [("gate", 0, 4)],
        [("branch", 0, 4)] + heads[2] + merge(0, 5),
        merge(0, 6) + merge(0, 7)])
    for h, u in enumerate((("ck", 0), ("cv", 0), ("cq", 0))):
        steps.append(("turn_out", h))
        unit(*u)
    steps.extend([("values", "c"), ("turn_out", HEADS_B - 1)])
    unit("gate", 1, 0)
    attention("C", ("branch", 1, 0), [
        [("cq", 1)] + merge(1, 1) + [("gate", 1, 2)],
        [("branch", 1, 2), ("cq", 2)] + merge(1, 3) + [("gate", 1, 4)],
        [("branch", 1, 4), ("cq", 3)] + merge(1, 5),
        merge(1, 6) + merge(1, 7)])
    return steps


def scalar_order(steps):
    steps = [s for s in steps if s[0] != "norm"]
    for n in range(1, len(steps)):
        if steps[n][0] == "turn" and steps[n][2] == 1:
            if steps[n - 1][0] == "unit":
                steps[n - 1:n + 1] = steps[n], steps[n - 1]
            elif steps[n - 2][0] == "exp":
                steps[n - 2:n + 1] = steps[n - 1], steps[n], steps[n - 2]
    return steps


STEPS = [mixer_steps(l) for l in range(DEPTH)]
UNITS = [s[1] for s in STEPS[0] if s[0] == "unit"]
assert len(UNITS) % 2 == 0 and all([s[1] for s in steps if s[0] == "unit"] == UNITS for steps in STEPS)


PLACE = {u: n for n, u in enumerate(UNITS)}


def tiles_after(u):
    after = PLACE[u] + 2 - len(UNITS)
    return (NT, KM)[after] if after >= 0 else tiles_of(UNITS[after])


FILL = {(l, *s): n + 1 for n, (l, s) in enumerate(
    (l, s) for l in range(DEPTH) for s in STEPS[l]
    if s[0] in ("rowsum", "vn", "mix", "values", "turn", "out", "turn_out"))}
ROUND = {(l, s[1]): n + 1 for n, (l, s) in enumerate(
    (l, s) for l in range(DEPTH) for s in STEPS[l] if s[0] == "scores")}
ADA_IN_UNIT = dict(zip(UNITS, (1, 2, 2, 1, 1, 1, 2, 2)))
assert sum(ADA_IN_UNIT.values()) == ADA_START - 2 * NT


def sums_before(l):
    return NT + 2 * NT * l


def width(l):
    return TOK if l < DEPTH - 1 else SEQ


def hybrid_prefix_dit_block(nc, t):
    ctx = ExitStack()
    with ctx:
        def sb(name, shape, dt=F32, scope=ctx):
            return scope.enter_context(nc.sbuf_tensor(name, shape, dt))

        def pb(name, shape):
            return ctx.enter_context(nc.psum_tensor(name, shape, F32))

        def sem(name):
            return ctx.enter_context(nc.semaphore(name))

        with ExitStack() as spill:
            QT = [sb(f"QT{i}", [P, 2, TOK], F32R, spill) for i in range(2)]
            KH = [sb("KH0", [P, 2, TOK], F32R, spill)]
            with ExitStack() as windowed:
                AT1 = sb("AT1", [P, NBLK, P], F32, windowed)
            KH.append(sb("KH1", [P, 2, TOK], F32R, spill))
        X = sb("X", [P, NT, TOK])
        x_dram = nc.dram_tensor("x_dram", (P, NT, TOK), F32).ap()
        Hhi, Hlo = sb("Hhi", [P, NT, TOK], F32R), sb("Hlo", [P, NT, TOK], F32R)
        raw = sb("raw", [P, 2, SLOT])
        Whi = [sb(f"Whi{s}", [P, SLOT], F32R) for s in range(2)]
        Wlo = [sb(f"Wlo{s}", [P, SLOT], F32R) for s in range(2)]
        consts, ones = sb("consts", [P, C_END]), sb("ones", [P, P])
        vecs = [sb(f"vecs{l}", [P, V_END]) for l in range(DEPTH)]
        mod = [sb(f"mod{l}", [P, 6, NT, 2]) for l in range(DEPTH)]
        gain = [sb(f"gain{i}", [P, NT, 2]) for i in range(2)]
        cond_in = sb("cond_in", [P, 2, NT])
        cond = sb("cond", [P, NT, 2])
        adasum = sb("adasum", [P, ADA_UNITS, 2])
        adacol = sb("adacol", [P, 2])
        final_gain = sb("final_gain", [P, NT])
        small = sb("small", [P, 64])
        eps_col = sb("eps_col", [P, 1])
        sqacc = sb("sqacc", [P, TOK])
        tmp = sb("tmp", [P, 2, TOK])
        cos, sin = consts[:, C_COS:C_COS + SEQ], consts[:, C_SIN:C_SIN + SEQ]
        ident = consts[:, C_ID:C_ID + P]
        mask_prev, mask_next = consts[:, C_PREV:C_PREV + P], consts[:, C_NEXT:C_NEXT + P]

        with ExitStack() as mix:
            with ExitStack() as first_ada:
                adaw = [sb("adaw0", [P, 4, D_MODEL], F32, first_ada)]
                condb = [sb("condb0", [P, 2, D_MODEL], F32, first_ada)]
            Y = sb("Y", [P, NT, TOK], F32, mix)
            Ohi, Olo = sb("Ohi", [P, KM, TOK], F32R, mix), sb("Olo", [P, KM, TOK], F32R, mix)
            with ExitStack() as second_ada:
                adaw.append(sb("adaw1", [P, 2, D_MODEL], F32, second_ada))
                condb.append(sb("condb1", [P, 2, D_MODEL], F32, second_ada))
            with ExitStack() as start:
                ada_first = sb("ada_first", [P, ADA_PE, D_MODEL], F32, start)
            KL, V = [sb("KL0", [P, 2, TOK], F32R, mix)], [sb("V0", [P, NBLK, P], F32, mix)]
            with ExitStack() as gating:
                U = sb("U", [P, KM, TOK], F32, gating)
                VN = sb("VN", [P, NBLK, MIX_W], F32, gating)
                VF = sb("VF", [P, TOK], F32, gating)
                VF2 = sb("VF2", [P, TOK], F32, gating)
                wsT = sb("wsT", [P, KM, P], F32, gating)
                bs_rows = sb("bs_rows", [P, KM, P], F32, gating)
                bn = sb("bn", [P, NBLK, 6], F32, gating)
                lamv, lamp = sb("lamv", [P, 4, HEAD_DIM], F32, gating), sb("lamp", [P, 2, HEAD_DIM], F32, gating)
            KL.append(sb("KL1", [P, 2, TOK], F32R, mix))
            V.append(sb("V1", [P, NBLK, P], F32, mix))
            prob = [sb(f"prob{i}", [P, 2, TOK], F32, mix) for i in range(2)]
            AT = sb("AT", [P, NBLK, P], F32, mix)
            Oraw = sb("Oraw", [P, KM * TOK], F32, mix)
            stat = [sb(f"stat{i}", [P, 24], F32, mix) for i in range(2)]
            square = sb("square", [P, P], F32, mix)
        Otok = Oraw[:, :].rearrange("p (b f) -> p b f", f=MIX_W)
        Ofeat = Oraw[:, :].rearrange("p (t q) -> p t q", q=TOK)
        turned = [AT, AT1]
        mixed_buf = [VF[:, :], VF2[:, :]]

        VT = sqacc

        with ExitStack() as ffn:
            Ghi, Glo = sb("Ghi", [P, NT, TOK], F32R, ffn), sb("Glo", [P, NT, TOK], F32R, ffn)
            apad = sb("apad", [P, TOK + 3], F32, ffn)
            conv, th = sb("conv", [P, TOK + 1], F32, ffn), sb("th", [P, TOK + 1], F32, ffn)
            adaw.append(sb("adaw2", [P, 1, D_MODEL], F32, ffn))
            condb.append(sb("condb2", [P, 2, D_MODEL], F32, ffn))
        diag = AT[:, :, :].rearrange("p k q -> p (k q)")

        psL = pb("psL", [P, 2, 512])
        psC = pb("psC", [P, 512])
        psS = pb("psS", [P, 2 * TOK])
        psT = pb("psT", [P, 1024])
        PV = slice(TOK, TOK + P)
        RSTD = slice(512, 512 + TOK)
        SUMS = 0
        JUNK = slice(512, 512 + D_MODEL)
        maps = psS[:, :].rearrange("p (m c) -> p m c", m=2)

        loaded = [sem(f"loaded{s}") for s in range(2)]
        raw_read = [sem(f"raw_read{s}") for s in range(2)]
        consts_loaded, x_loaded, cond_loaded, vecs_loaded, gating_loaded, stored = (sem(n) for n in (
            "consts_loaded", "x_loaded", "cond_loaded", "vecs_loaded", "gating_loaded", "stored"))
        ones_ready, cond_ready, mod_ready, pads_ready, fin_ready = (sem(n) for n in (
            "ones_ready", "cond_ready", "mod_ready", "pads_ready", "fin_ready"))
        hi_ready = sem("hi_ready")
        lat_done, ctx_done = sem("lat_done"), sem("ctx_done")
        lat_read, ctx_read = [sem(f"lat_read{s}") for s in range(2)], sem("ctx_read")
        act_step, dve_step = sem("act_step"), sem("dve_step")
        sq_ready, acc_ready, sum_done, std_ready, diag_ready, rstd_done = (sem(n) for n in (
            "sq_ready", "acc_ready", "sum_done", "std_ready", "diag_ready", "rstd_done"))
        xn_ready, h_hi, h_ready = sem("xn_ready"), sem("h_hi"), sem("h_ready")
        t_done, t_read = sem("t_done"), sem("t_read")
        ln_var, ln_std, ln_ready = sem("ln_var"), sem("ln_std"), sem("ln_ready")
        oc_hi, oc_ready = sem("oc_hi"), sem("oc_ready")
        mixed, mixed_hi, mixed_ready = sem("mixed"), sem("mixed_hi"), sem("mixed_ready")
        y_ready = sem("y_ready")
        rotated, qk_hi, qk_ready = sem("rotated"), sem("qk_hi"), sem("qk_ready")
        x_spilled, x_back = sem("x_spilled"), sem("x_back")
        scores_done, bias_ready, exp_done, prob_ready = (sem(n) for n in (
            "scores_done", "bias_ready", "exp_done", "prob_ready"))
        head_std, head_ready, o_hi = sem("head_std"), sem("head_ready"), sem("o_hi")
        conv_ready, th_ready, g_hi, g_ready = (sem(n) for n in ("conv_ready", "th_ready", "g_hi", "g_ready"))
        ada_loaded = [sem(f"ada_loaded{s}") for s in range(4)]
        ada_first_loaded = [sem(f"ada_first_loaded{g}") for g in range(ADA_PE // ADA_GROUP)]
        ada_done = sem("ada_done")
        ada_read, condb_loaded, condb_ready = sem("ada_read"), sem("condb_loaded"), sem("condb_ready")
        ada_copied = sem("ada_copied")
        lam_loaded, condb0_loaded = sem("lam_loaded"), sem("condb0_loaded")
        lam_dot, lam_exp = sem("lam_dot"), sem("lam_exp")

        LAMSUM, LAMEXP, NEGLAM, SUBG, NEGSINK, SINK, XSTD, XREC, LNMV, LNSTD, WARM = 0, 2, 4, 5, 8, 16, 24, 30, 36, 48, 54
        MX, NB, SUM, REC, SINKB, SINKE, SSQ, HSTD = 0, 2, 4, 6, 8, 10, 12, 18
        assert HSTD + NBLK <= 24

        block = ctx.enter_context(nc.Block())

        @block.sync
        def _(sp):
            n_load = [Count(), Count()]

            def load(slot, src, nk):
                if n_load[slot].begun():
                    sp.wait_ge(raw_read[slot], n_load[slot].now())
                sp.dma_start(raw[:, slot, 0:nk * P], src).then_inc(loaded[slot], 16)
                n_load[slot].up()

            def pairs(times, slot, first, second):
                with loop(sp, times, {n_load[0]: 1, n_load[1]: 1}) as i:
                    load(slot, *first(i))
                    load(1 - slot, *second(i))

            def unit_source(l, u):
                if u[0] == "gate":
                    return t["w_in"][l, len(KINDS) + u[1] * NT + u[2]]
                if u[0] == "branch":
                    return t["w_branch"][l, u[1] * NT + u[2]]
                return t["w_in"][l, KINDS.index(u)]

            def load_ada(g):
                us = slice(g * ADA_GROUP, (g + 1) * ADA_GROUP)
                sp.dma_start(ada_first[:, us, :], t["w_ada_first"][:, us, :]).then_inc(ada_first_loaded[g], 16)

            sp.dma_start(cond_in[:, 0, :], t["c"]).then_inc(cond_loaded, 16)
            sp.dma_start(cond_in[:, 1, :], t["c_ctx"]).then_inc(cond_loaded, 16)
            sp.dma_start(condb[0][:, 0, :], t["c_row"].partition_broadcast(P)).then_inc(condb0_loaded, 16)
            sp.dma_start(condb[0][:, 1, :], t["c_ctx_row"].partition_broadcast(P)).then_inc(condb0_loaded, 16)
            load_ada(0)
            sp.dma_start(X[:, :, LAT], t["x"]).then_inc(x_loaded, 16)
            load_ada(1)
            sp.dma_start(X[:, :, CT], t["ctx"]).then_inc(x_loaded, 16)
            load_ada(2)
            sp.dma_start(vecs[0][:, :], t["vecs"][0]).then_inc(vecs_loaded, 16)
            sp.dma_start(consts[:, :], t["consts"]).then_inc(consts_loaded, 16)
            sp.dma_start(vecs[1][:, :], t["vecs"][1]).then_inc(vecs_loaded, 16)
            sp.dma_start(final_gain[:, :], t["final_g"]).then_inc(consts_loaded, 16)
            for l in range(DEPTH):
                for n, u in enumerate(UNITS[:2]):
                    load(n, unit_source(l, u), tiles_of(u))
                if l:
                    sp.wait_ge(acc_ready, sums_before(l))
                sp.dma_start(lamv[:, :, :], t["lam"][l].partition_broadcast(P)).then_inc(lam_loaded, 16)
                sp.dma_start(small[:, SINK:SINK + 8], t["sinks"][l].partition_broadcast(P)).then_inc(lam_loaded, 16)
                sp.dma_start(wsT[:, :, :], t["w_s"][l]).then_inc(gating_loaded, 16)
                sp.dma_start(bs_rows[:, :, :], t["b_s"][l].partition_broadcast(P)).then_inc(gating_loaded, 16)
                for n, u in enumerate(UNITS[2:]):
                    load(n % 2, unit_source(l, u), tiles_of(u))
                pairs(NT, 0, lambda n: (t["w_in"][l, n + (len(KINDS) + 2 * NT)], NT),
                      lambda n: (t["w_branch"][l, n + 2 * NT], KM))
                pairs(NT // 2, 0, lambda i: (t["w_out"][l, 2 * i], NT), lambda i: (t["w_out"][l, 2 * i + 1], NT))
                for f, tiles in PARTS:
                    pairs(tiles, 0, lambda i: (t["w_gate"][l, i + f], NT), lambda i: (t["w_up"][l, i + f], NT))
                    part = slice(f * P, (f + tiles) * P)
                    pairs(NT // 2, 0, lambda i: (t["w_down"][l, 2 * i, :, part], tiles),
                          lambda i: (t["w_down"][l, 2 * i + 1, :, part], tiles))
            for n in range(NT):
                sp.wait_ge(fin_ready, n + 1)
                sp.dma_start(t["out"][:, n, :], X[:, n, LAT]).then_inc(stored, 16)
            sp.wait_ge(stored, 16 * NT)

        @block.gpsimd
        def _(pool):
            nc.gpsimd.memset(ones[:, :], 1.0).then_inc(ones_ready, 1)
            nc.gpsimd.memset(eps_col[:, :], EPS).then_inc(ones_ready, 1)

            def spill_x(l):
                pool.wait_ge(h_ready, 3 * NT * l + NT)
                pool.dma_start(x_dram[:, :, 0:width(l)], X[:, :, 0:width(l)]).then_inc(x_spilled, 16)

            def x_from_dram(l):
                pool.wait_ge(t_done, FILL[(l, *STEPS[l][-1])])
                pool.wait_ge(x_spilled, 16 * (l + 1))
                pool.dma_start(X[:, :, 0:width(l)], x_dram[:, :, 0:width(l)]).then_inc(x_back, 16)

            for n in range(ADA_START - ADA_PE):
                if n == 2 * NT - ADA_PE + 4:
                    spill_x(0)
                if n >= 4:
                    pool.wait_ge(ada_read, n - 3)
                pool.dma_start(adaw[0][:, n % 4, :], t["w_ada_rows"][0, n + ADA_PE]).then_inc(ada_loaded[n % 4], 16)
            pool.wait_ge(t_done, FILL[(0, *STEPS[0][-1])])
            used = ADA_START - ADA_PE
            pool.dma_start(condb[1][:, 0, :], t["c_row"].partition_broadcast(P)).then_inc(condb_loaded, 16)
            pool.dma_start(condb[1][:, 1, :], t["c_ctx_row"].partition_broadcast(P)).then_inc(condb_loaded, 16)
            x_from_dram(0)
            for n in range(ADA_UNITS - ADA_START):
                if n >= 2:
                    pool.wait_ge(ada_read, used + n - 1)
                pool.dma_start(adaw[1][:, n % 2, :], t["w_ada_rows"][0, ADA_START + n]).then_inc(ada_loaded[n % 2], 16)
            used += ADA_UNITS - ADA_START
            for l in range(DEPTH):
                if l:
                    spill_x(l)
                    x_from_dram(l)
                pool.wait_ge(rstd_done, sum(3 + (k < DEPTH - 1) for k in range(l + 1)))
                nc.gpsimd.memset(apad[:, 0:1], 0.0)
                nc.gpsimd.memset(apad[:, SEQ + 1:SEQ + 2], 0.0)
                nc.gpsimd.memset(apad[:, TOK + 2:TOK + 3], 0.0).then_inc(pads_ready, 1)
                if l == 0:
                    pool.dma_start(condb[2][:, 0, :], t["c_row"].partition_broadcast(P)).then_inc(condb_loaded, 16)
                    pool.dma_start(condb[2][:, 1, :], t["c_ctx_row"].partition_broadcast(P)).then_inc(condb_loaded, 16)
                    for n in range(ADA_UNITS):
                        if n:
                            pool.wait_ge(ada_read, used + n)
                        pool.dma_start(adaw[2][:, 0, :], t["w_ada_rows"][1, n]).then_inc(ada_loaded[0], 16)

        @block.tensor
        def _(pe):
            n_unit, n_lat, n_ctx, n_load, n_h = Count(), [Count(), Count()], Count(), [Count(), Count()], Count()
            n_qk, n_norm = Count(), Count()

            def products(slot, nk, hi, lo, part, k0, k1, lo_ready=None):
                out = psC[:, 0:CTX] if part else psL[:, slot, :]
                cols = CT if part else LAT
                for k in range(k0, k1):
                    w = slice(k * P, (k + 1) * P)
                    nc.tensor.matmul(out, Whi[slot][:, w], hi[:, k, cols], start=(k == 0), stop=False)
                    nc.tensor.matmul(out, Wlo[slot][:, w], hi[:, k, cols], start=False, stop=False)
                    if lo_ready:
                        pe.wait_ge(*lo_ready)
                    mm = nc.tensor.matmul(out, Whi[slot][:, w], lo[:, k, cols], start=False, stop=(k == nk - 1))
                if k1 == nk:
                    mm.then_inc(ctx_done if part else lat_done, 1)

            def begin(slot):
                pe.wait_ge(hi_ready, n_unit.up())
                pe.wait_ge(raw_read[slot], n_load[slot].up())
                if n_lat[slot].begun():
                    pe.wait_ge(lat_read[slot], n_lat[slot].now())
                n_lat[slot].up()

            def first_half(slot, nk, hi, lo, ctx_too):
                begin(slot)
                products(slot, nk, hi, lo, 0, 0, nk * 3 // 4 if ctx_too else nk // 2)

            def second_half(slot, nk, hi, lo, ctx_too):
                products(slot, nk, hi, lo, 0, nk * 3 // 4 if ctx_too else nk // 2, nk)
                if ctx_too:
                    if n_ctx.begun():
                        pe.wait_ge(ctx_read, n_ctx.now())
                    n_ctx.up()
                    products(slot, nk, hi, lo, 1, 0, nk)

            def unit(slot, nk, hi, lo, ctx_too):
                first_half(slot, nk, hi, lo, ctx_too)
                second_half(slot, nk, hi, lo, ctx_too)

            def two_units(ctx_too):
                begin(0)
                if ctx_too and n_ctx.begun():
                    pe.wait_ge(ctx_read, n_ctx.now())
                start, held = 3, 5
                for k in range(NT):
                    pe.wait_ge(h_hi, n_h.up())
                    products(0, NT, Hhi, Hlo, 0, k, k + 1, (h_ready, n_h.now()))
                    if ctx_too:
                        products(0, NT, Hhi, Hlo, 1, k, k + 1)
                    if k == start:
                        begin(1)
                        products(1, NT, Hhi, Hlo, 0, 0, start)
                    if start <= k < held:
                        products(1, NT, Hhi, Hlo, 0, k, k + 1)
                products(1, NT, Hhi, Hlo, 0, held, NT)
                if ctx_too:
                    pe.wait_ge(ctx_read, n_ctx.up())
                    products(1, NT, Hhi, Hlo, 1, 0, NT)
                    n_ctx.up()

            def first_down(tiles, base, ctx_too):
                begin(0)
                for k in range(tiles):
                    pe.wait_ge(g_hi, base + k + 1)
                    products(0, tiles, Ghi, Glo, 0, k, k + 1, (g_ready, base + k + 1))
                if ctx_too:
                    pe.wait_ge(ctx_read, n_ctx.now())
                    n_ctx.up()
                    products(0, tiles, Ghi, Glo, 1, 0, tiles)

            def psT_free(fill):
                if FILL[fill] > 1:
                    pe.wait_ge(t_read, FILL[fill] - 1)

            def turn(fill, tiles):
                psT_free(fill)
                for k, src in enumerate(tiles):
                    mm = nc.tensor.transpose(psT[:, k * P:(k + 1) * P], src, ident)
                mm.then_inc(t_done, 1)

            def norm_sums(ready, tok):
                pe.wait_ge(acc_ready, ready)
                for b in range(tok // P):
                    mm = nc.tensor.matmul(psS[:, SUMS + b:SUMS + b + 1], sqacc[:, b * P:(b + 1) * P], ones[:, 0:1],
                                          start=True, stop=True)
                mm.then_inc(sum_done, 1)
                pe.wait_ge(diag_ready, n_norm.up())
                for cols in (LAT, CT)[:1 + (tok > SEQ)]:
                    nc.tensor.matmul(psS[:, RSTD][:, cols], ones[:, :], diag[:, cols],
                                     start=True, stop=True).then_inc(rstd_done, 1)

            def scores(l, kind, h, b):
                if ROUND[l, (kind, h, b)] > 1:
                    pe.wait_ge(exp_done, ROUND[l, (kind, h, b)] - 1)
                elif l == 0:
                    pe.wait_ge(ada_read, ADA_START - ADA_PE)
                if b == 0:
                    pe.wait_ge(qk_ready, n_qk.up(2 if kind == "B" or h == 0 else 1))
                i = h % 2 if kind == "B" else 0
                for m in range(2):
                    q = QT[h % 2][:, m, b * P:(b + 1) * P]
                    for dst, src, n in key_runs(m, key_blocks(kind, b)):
                        out = psS[:, dst:dst + n]
                        nc.tensor.matmul(out, q, KH[i][:, m, src:src + n], start=True, stop=False, skip_group_check=True)
                        mm = nc.tensor.matmul(out, q, KL[i][:, m, src:src + n], start=False, stop=True,
                                              skip_group_check=True)
                mm.then_inc(scores_done, 1)

            evacuated = {}

            def out_of_psum(*u):
                lat, context = evacuated[u]
                pe.wait_ge(lat_read[PLACE[u] % 2], lat)
                pe.wait_ge(ctx_read, context)

            def products_with_values(l, kind, h, b):
                keys = key_blocks(kind, b)
                psT_free((l, "out", (kind, h, b)))
                for m in range(1 if kind == "B" else 2):
                    rows = slice(m * HEAD_DIM, (m + 1) * HEAD_DIM)
                    for k, kb in enumerate(keys):
                        flags = dict(start=(k == 0), stop=(k == len(keys) - 1))
                        if kind == "B":
                            mm = nc.tensor.matmul(psT[:, PV], turned[0][:, k, :], V[h % 2][:, kb, :], **flags)
                        else:
                            mm = nc.tensor.matmul(psT[rows, PV], V[0][:, kb, rows], turned[m][:, k, :], **flags)
                mm.then_inc(t_done, 1)

            def mixers(l):
                blocks = blocks_of(l)
                two_units(l < DEPTH - 1)
                for s in range(2):
                    evacuated[UNITS[s]] = (n_lat[s].now(), n_ctx.now(1 - s if l < DEPTH - 1 else 0))
                for step in STEPS[l][4:]:
                    what, arg = step[0], step[1] if len(step) > 1 else None
                    fill = (l, *step)
                    if what in ("half", "unit"):
                        slot, nk = PLACE[arg] % 2, tiles_of(arg)
                        source = (Ohi, Olo) if arg[0] == "branch" else (Hhi, Hlo)
                        if arg == ("branch", 0, 0):
                            pe.wait_ge(mixed_ready, KM * (l + 1))
                        if arg == ("branch", 1, 0):
                            pe.wait_ge(t_read, FILL[l, "turn_out", HEADS_B - 1])
                        if what == "half":
                            first_half(slot, nk, *source, with_ctx(arg, l))
                        else:
                            second_half(slot, nk, *source, with_ctx(arg, l))
                            evacuated[arg] = (n_lat[slot].now(), n_ctx.now())
                    elif what == "rowsum":
                        pe.wait_ge(gating_loaded, 32 * (l + 1))
                        pe.wait_ge(mod_ready, 1)
                        psT_free(fill)
                        nc.tensor.matmul(psT[:, 0:MIX_W], ones[:, :], wsT[:, :, :].rearrange("p g q -> p (g q)"),
                                         start=True, stop=True).then_inc(t_done, 1)
                    elif what == "vn":
                        out_of_psum("a", arg)
                        turn(fill, [mixed_buf[arg % 2][:, k * P:(k + 1) * P] for k in range(blocks)])
                    elif what == "values":
                        out_of_psum("cv", 0) if arg == "c" else out_of_psum("v", arg)
                        turn(fill, [VT[:, k * P:(k + 1) * P] for k in range(NBLK)])
                    elif what == "mix":
                        pe.wait_ge(ln_ready, l + 1)
                        psT_free(fill)
                        for b in range(blocks):
                            mm = nc.tensor.matmul(psT[:, b * P:(b + 1) * P], VN[:, b, arg * P:(arg + 1) * P],
                                                  wsT[:, arg, :], start=True, stop=True, skip_group_check=True)
                        mm.then_inc(t_done, 1)
                    elif what == "scores":
                        scores(l, *arg)
                    elif what == "turn":
                        pe.wait_ge(prob_ready, ROUND[l, arg])
                        pr = prob[ROUND[l, arg] % 2]
                        turn(fill, [pr[:, step[2], k * P:(k + 1) * P] for k in range(len(key_blocks(arg[0], arg[2])))])
                    elif what == "out":
                        products_with_values(l, *arg)
                    elif what == "turn_out":
                        pe.wait_ge(head_ready, HEADS_B * l + arg + 1)
                        turn(fill, [Otok[:, k, arg * P:(arg + 1) * P] for k in range(blocks)])

            pe.wait_ge(cond_ready, 1)

            for u in range(ADA_PE):
                pe.wait_ge(ada_first_loaded[u // ADA_GROUP], 16)
                for k in range(NT):
                    mm = nc.tensor.matmul(psT[:, 2 * u:2 * u + 2], ada_first[:, u, k * P:(k + 1) * P], cond[:, k, :],
                                          start=(k == 0), stop=(k == NT - 1))
            mm.then_inc(ada_done, 1)
            pe.wait_ge(ones_ready, 2)
            pe.wait_ge(consts_loaded, 32)
            for l in range(DEPTH):
                c = l < DEPTH - 1
                per_pair = {n_unit: 2, n_lat[0]: 1, n_lat[1]: 1, n_load[0]: 1, n_load[1]: 1, n_ctx: 2 * c}
                if l:
                    pe.wait_ge(mod_ready, l + 1)
                norm_sums(sums_before(l), TOK)
                mixers(l)
                with loop(pe, NT, per_pair):
                    unit(0, NT, Hhi, Hlo, c)
                    pe.wait_ge(oc_ready, KM * (l + 1))
                    unit(1, KM, Ohi, Olo, c)
                two_units(c)
                with loop(pe, NT // 2 - 1, per_pair):
                    unit(0, NT, Hhi, Hlo, c)
                    unit(1, NT, Hhi, Hlo, c)
                norm_sums(sums_before(l) + NT, width(l))
                for f, tiles in PARTS:
                    if f == 0:
                        two_units(c)
                    with loop(pe, tiles - (f == 0), per_pair):
                        unit(0, NT, Hhi, Hlo, c)
                        unit(1, NT, Hhi, Hlo, c)
                    base = NF * l + f
                    first_down(tiles, base, c)
                    unit(1, tiles, Ghi, Glo, c)
                    with loop(pe, NT // 2 - 1, per_pair):
                        unit(0, tiles, Ghi, Glo, c)
                        unit(1, tiles, Ghi, Glo, c)
            norm_sums(sums_before(DEPTH), SEQ)

        @block.scalar
        def _(act):
            n_lat, n_ctx, n_load, n_step = Count(), Count(), [Count(), Count()], Count()
            n_slot = [Count(), Count()]
            n_sq, n_norm, n_xn, n_conv, n_qk, n_split = (Count() for _ in range(6))

            def link(ins):
                ins.then_inc(act_step, 1)
                act.wait_ge(act_step, n_step.up())

            def split(slot, nk):
                act.wait_ge(loaded[slot], n_load[slot].up() * 16)
                if n_lat.begun():
                    act.wait_ge(lat_done, n_lat.now())
                if n_ctx.begun():
                    act.wait_ge(ctx_done, n_ctx.now())
                nc.scalar.activation(Whi[slot][:, 0:nk * P], raw[:, slot, 0:nk * P], ACT.Copy).then_inc(hi_ready, 1)

            def passed(slot, ctx_too, next_nk):
                n_lat.up()
                n_slot[slot].up()
                if ctx_too:
                    n_ctx.up()
                if next_nk:
                    split(slot, next_nk)

            def take(slot, ctx_too, lat_out, ctx_out, func, scale=1.0):
                act.wait_ge(lat_done, n_lat.now())
                nc.scalar.activation(lat_out, psL[:, slot, :], func, scale=scale).then_inc(lat_read[slot], 1)
                if ctx_too:
                    act.wait_ge(ctx_done, n_ctx.now())
                    nc.scalar.activation(ctx_out, psC[:, 0:CTX], func, scale=scale).then_inc(ctx_read, 1)

            def square_tile(n, slot, w):
                n_sq.up()
                if n_sq.i is not None or n_sq.n > 2:
                    act.wait_ge(acc_ready, n_sq.now(2))
                nc.scalar.activation(tmp[:, slot, 0:w], X[:, n, 0:w], ACT.Square).then_inc(sq_ready, 1)

            def updated(slot, ctx_too):
                act.wait_ge(lat_read[slot], n_slot[slot].now())
                if ctx_too:
                    act.wait_ge(ctx_read, n_ctx.now())

            def rms(tok):
                nc.scalar.activation(small[:, WARM:WARM + 1], eps_col[:, :], ACT.Sqrt)
                act.wait_ge(sum_done, n_norm.up())
                nc.scalar.activation(small[:, XSTD:XSTD + tok // P], psS[:, SUMS:SUMS + tok // P], ACT.Sqrt,
                                     scale=1.0 / D_MODEL, bias=eps_col[:, :]).then_inc(std_ready, 1)

            def norm(l, tok, shift):
                rms(tok)
                for n in range(NT):
                    act.wait_ge(xn_ready, n_xn.up())
                    for m, cols in enumerate((LAT, CT)[:1 + (tok > SEQ)]):
                        ins = nc.scalar.activation(Hhi[:, n, cols], tmp[:, n % 2, cols], ACT.Identity,
                                                   bias=mod[l][:, shift, n, m:m + 1])
                    ins.then_inc(h_hi, 1)

            def mixers(l):
                nb, w = blocks_of(l), width(l)
                for step in scalar_order(STEPS[l]):
                    what, arg = step[0], step[1] if len(step) > 1 else None
                    fill = (l, *step)
                    if what == "unit":
                        input_unit(l, arg)
                    elif what == "ln":
                        act.wait_ge(ln_var, l + 1)
                        nc.scalar.activation(small[:, LNSTD:LNSTD + nb],
                                             small[:, LNMV:LNMV + 2 * nb].rearrange("p (b s) -> p b s", s=2)[:, :, 1],
                                             ACT.Sqrt, bias=eps_col[:, :]).then_inc(ln_std, 1)
                    elif what == "mix":
                        act.wait_ge(mixed, KM * l + arg + 1)
                        nc.scalar.activation(Ohi[:, arg, 0:w], mixed_buf[arg % 2][:, 0:w], ACT.Copy).then_inc(mixed_hi, 1)
                    elif what == "split_qk":
                        n_split.up()
                        act.wait_ge(rotated, n_split.now())
                        act.wait_ge(x_spilled, 16 * (l + 1))
                        w_qk = TOK if with_ctx(arg, l) else SEQ
                        keys = arg[0] in ("k", "ck")
                        for m in range(2):
                            own, other = slice(m * 64, m * 64 + 64), slice(64 - m * 64, 128 - m * 64)
                            for to in (own, other) if keys else (own,):
                                ins = nc.scalar.activation((KH if keys else QT)[arg[1] % 2][to, m, 0:w_qk],
                                                           tmp[own, 1, 0:w_qk], ACT.Copy)
                        ins.then_inc(qk_hi, 1)
                    elif what == "values":
                        act.wait_ge(t_done, FILL[fill])
                        nc.scalar.activation(V[0 if arg == "c" else arg % 2][:, :, :], psT[:, 0:TOK].rearrange(
                            "p (k q) -> p k q", q=P), ACT.Copy).then_inc(t_read, 1)
                    elif what == "exp":
                        exps(l, arg)
                    elif what == "turn":
                        nk = len(key_blocks(arg[0], arg[2]))
                        act.wait_ge(t_done, FILL[fill])
                        nc.scalar.activation(turned[step[2]][:, 0:nk, :], psT[:, 0:nk * P].rearrange(
                            "p (k q) -> p k q", q=P), ACT.Copy).then_inc(t_read, 1)
                    elif what == "out":
                        attention_out(l, fill, *arg)
                    elif what == "turn_out":
                        act.wait_ge(t_done, FILL[fill])
                        nc.scalar.activation(Ohi[:, arg, 0:w], psT[:, 0:w], ACT.Copy,
                                             scale=small[:, SUBG:SUBG + 1]).then_inc(o_hi, 1)

            def exps(l, r):
                st = stat[ROUND[l, r] % 2]
                nk = len(key_blocks(r[0], r[2])) * P
                act.wait_ge(bias_ready, ROUND[l, r])
                if r[0] == "C":
                    nc.scalar.activation(st[:, SINKE:SINKE + 2], st[:, SINKB:SINKB + 2], ACT.Exp)
                for m in range(2):
                    ins = nc.scalar.activation(prob[ROUND[l, r] % 2][:, m, 0:nk], psS[:, m * TOK:m * TOK + nk], ACT.Exp,
                                               scale=SCALE, bias=st[:, NB + m:NB + m + 1],
                                               accum_out=st[:, SUM + m:SUM + m + 1])
                ins.then_inc(exp_done, 1)

            def attention_out(l, fill, kind, h, b):
                nb = blocks_of(l)
                act.wait_ge(t_done, FILL[fill])
                if kind == "C":
                    nc.scalar.activation(Ofeat[:, h, b * P:(b + 1) * P], psT[:, PV], ACT.Copy).then_inc(t_read, 1)
                    return
                nc.scalar.activation(square[:, :], psT[:, PV], ACT.Square, accum_out=stat[0][:, SSQ + b:SSQ + b + 1])
                nc.scalar.activation(Otok[:, b, h * P:(h + 1) * P], psT[:, PV], ACT.Copy).then_inc(t_read, 1)
                if b == nb - 1:
                    act.wait_ge(t_read, FILL[fill])
                    nc.scalar.activation(stat[0][:, HSTD:HSTD + nb], stat[0][:, SSQ:SSQ + nb], ACT.Sqrt,
                                         scale=1.0 / P, bias=eps_col[:, :]).then_inc(head_std, 1)

            def input_unit(l, u):
                kind, c, slot = u[0], with_ctx(u, l), PLACE[u] % 2
                if kind == "gate":
                    updated(1 - slot, True)
                passed(slot, c, tiles_after(u))
                if kind == "u":
                    take(slot, c, U[:, u[1], LAT], U[:, u[1], CT], ACT.Gelu_apprx_tanh)
                elif kind == "a":
                    if u[1] > 1:
                        act.wait_ge(t_done, FILL[l, "vn", u[1] - 2])
                    out = mixed_buf[u[1] % 2]
                    take(slot, c, out[:, LAT], out[:, CT], ACT.Gelu_apprx_tanh)
                elif kind in ("v", "cv"):
                    take(slot, c, VT[:, LAT], VT[:, CT], ACT.Copy)
                elif kind == "gate":
                    act.wait_ge(rotated, n_qk.now())
                    take(slot, c, tmp[:, 0, LAT], tmp[:, 0, CT], ACT.Tanh, 0.5)
                elif kind != "branch":
                    n_qk.up()

            def y_hi(l, n):
                act.wait_ge(y_ready, 2 * NT * l + NT + n + 1)
                nc.scalar.activation(Hhi[:, n, 0:width(l)], Y[:, n, 0:width(l)], ACT.Copy, scale=0.5).then_inc(h_hi, 1)

            def merge_tile(l, next_nk):
                c = l < DEPTH - 1
                updated(1, c)
                passed(0, c, NT)
                take(0, c, tmp[:, 0, LAT], tmp[:, 0, CT], ACT.Tanh, 0.5)
                passed(1, c, next_nk)

            def x_tile(l, n, slot, next_nk, squares, last=False):
                c = l < DEPTH - 1
                passed(slot, c, None if last else next_nk)
                if squares:
                    updated(slot, c)
                    square_tile(n, slot, width(l))
                if last and next_nk:
                    split(slot, next_nk)

            def ffn_tile(l, i, next_nk):
                c = l < DEPTH - 1
                w = TOK + 1 if c else SEQ
                passed(0, c, next_nk)
                if n_conv.begun():
                    act.wait_ge(conv_ready, n_conv.now())
                take(0, c, apad[:, 1:SEQ + 1], apad[:, SEQ + 2:TOK + 2], ACT.Copy)
                act.wait_ge(conv_ready, n_conv.up())
                nc.scalar.activation(th[:, 0:w], conv[:, 0:w], ACT.Tanh, scale=0.5).then_inc(th_ready, 1)
                passed(1, c, None)
                updated(1, c)
                nc.scalar.activation(Ghi[:, i, 0:width(l)], tmp[:, 0, 0:width(l)], ACT.Copy).then_inc(g_hi, 1)
                split(1, next_nk)

            act.wait_ge(cond_loaded, 32)
            nc.scalar.activation(cond[:, :, :].rearrange("p n m -> p m n"), cond_in[:, :, :],
                                 ACT.Silu).then_inc(cond_ready, 1)
            act.wait_ge(condb0_loaded, 32)
            nc.scalar.activation(condb[0][:, :, :], condb[0][:, :, :], ACT.Silu).then_inc(condb_ready, 1)
            act.wait_ge(x_loaded, 32)
            act.wait_ge(ones_ready, 2)
            for n in range(NT):
                square_tile(n, n % 2, TOK)
            for l in range(DEPTH):
                c = l < DEPTH - 1
                per_pair = {n_lat: 2, n_ctx: 2 * c, n_load[0]: 1, n_load[1]: 1, n_slot[0]: 1, n_slot[1]: 1}
                if l == 0:
                    split(0, NT)
                    split(1, NT)
                norm(l, TOK, 0)
                act.wait_ge(lam_dot, l + 1)
                nc.scalar.activation(small[:, LAMEXP:LAMEXP + 2], small[:, LAMSUM:LAMSUM + 2], ACT.Exp).then_inc(lam_exp, 1)
                mixers(l)
                act.wait_ge(lat_done, n_lat.now())
                if c:
                    act.wait_ge(ctx_done, n_ctx.now())
                act.wait_ge(t_read, FILL[(l, *STEPS[l][-1])])
                for h in range(PAIRS_C):
                    nc.scalar.activation(Ohi[:, h, 0:width(l)], Ofeat[:, h, 0:width(l)], ACT.Copy).then_inc(oc_hi, 1)
                if l == 0:
                    act.wait_ge(condb_loaded, 32)
                    nc.scalar.activation(condb[1][:, :, :], condb[1][:, :, :], ACT.Silu).then_inc(condb_ready, 1)
                with loop(act, NT - 1, per_pair):
                    merge_tile(l, KM)
                updated(1, c)
                passed(0, c, NT)
                take(0, c, tmp[:, 0, LAT], tmp[:, 0, CT], ACT.Tanh, 0.5)
                for n in range(3):
                    y_hi(l, n)
                passed(1, c, NT)
                for n in range(3, NT):
                    y_hi(l, n)
                with loop(act, NT // 2 - 1, per_pair | {n_sq: 2}) as i:
                    for s in range(2):
                        x_tile(l, 2 * i + s, s, NT, True)
                for n in (NT - 2, NT - 1):
                    x_tile(l, n, n % 2, NT, True, True)
                norm(l, width(l), 3)
                if l == 0:
                    act.wait_ge(condb_loaded, 64)
                    nc.scalar.activation(condb[2][:, :, :], condb[2][:, :, :], ACT.Silu).then_inc(condb_ready, 1)
                for f, tiles in PARTS:
                    with loop(act, tiles - 1, per_pair | {n_conv: 1}) as i:
                        ffn_tile(l, i, NT)
                    ffn_tile(l, tiles - 1, tiles)
                    squares = f == PARTS[-1][0]
                    with loop(act, NT // 2 - 1, per_pair | {n_sq: 2 * squares}) as i:
                        for s in range(2):
                            x_tile(l, 2 * i + s, s, tiles, squares)
                    for n in (NT - 2, NT - 1):
                        x_tile(l, n, n % 2, NT if l < DEPTH - 1 or not squares else None, squares, squares)
            rms(SEQ)

        @block.vector
        def _(dve):
            n_hi, n_lat, n_ctx, n_step = Count(), Count(), Count(), Count()
            n_slot = [Count(), Count()]
            n_acc, n_norm, n_hhi, n_ohi, n_th, n_ghi, n_qk, n_y, n_ada, n_rstd = (Count() for _ in range(10))
            n_ada_slot = [Count() for _ in range(4)]

            def link(ins):
                ins.then_inc(dve_step, 1)
                dve.wait_ge(dve_step, n_step.up())

            def split(slot, nk):
                dve.wait_ge(hi_ready, n_hi.up())
                nc.vector.tensor_tensor(Wlo[slot][:, 0:nk * P], raw[:, slot, 0:nk * P],
                                        Whi[slot][:, 0:nk * P].bitcast(F32), ALU.subtract).then_inc(raw_read[slot], 1)

            def passed(slot, ctx_too, next_nk):
                n_lat.up()
                n_slot[slot].up()
                if ctx_too:
                    n_ctx.up()
                if next_nk:
                    split(slot, next_nk)

            def lo_part(out, full, hi):
                return nc.vector.tensor_tensor(out, full, hi.bitcast(F32), ALU.subtract)

            def add_square(slot, w):
                dve.wait_ge(sq_ready, n_acc.up())
                nc.vector.tensor_tensor(sqacc[:, 0:w], sqacc[:, 0:w], tmp[:, slot, 0:w], ALU.add).then_inc(acc_ready, 1)
                dve.wait_ge(acc_ready, n_acc.now())

            def rms(tok):
                dve.wait_ge(std_ready, n_norm.up())
                nb = tok // P
                link(nc.vector.reciprocal(small[:, XREC:XREC + nb], small[:, XSTD:XSTD + nb]))
                nc.vector.tensor_tensor(diag[:, 0:tok].rearrange("p (b q) -> p b q", q=P),
                                        ident.unsqueeze(1).broadcast_to([P, nb, P]),
                                        small[:, XREC:XREC + nb].unsqueeze(2).broadcast_to([P, nb, P]),
                                        ALU.mult).then_inc(diag_ready, 1)

            def ada_unit(ring, u, slot, vectors):
                dve.wait_ge(ada_loaded[slot], n_ada_slot[slot].up() * 16)
                for m in range(vectors):
                    link(nc.vector.tensor_tensor_reduce(psS[:, JUNK], adaw[ring][:, slot, :], condb[ring][:, m, :],
                                                        1.0, 0.0, ALU.mult, ALU.add, adacol[:, m:m + 1]))
                nc.vector.tensor_copy(adasum[:, bass.ds(u, 1), 0:vectors],
                                      adacol[:, 0:vectors].unsqueeze(1)).then_inc(ada_read, 1)
                dve.wait_ge(ada_read, n_ada.up())

            def modulation(l, source, c0, c1, vectors):
                n = (c1 - c0) * NT
                return nc.vector.tensor_tensor(
                    mod[l][:, c0:c1, :, 0:vectors].rearrange("p c t m -> p (c t) m"), source,
                    vecs[l][:, V_ADA + c0 * NT:V_ADA + c1 * NT].unsqueeze(2).broadcast_to([P, n, vectors]), ALU.add)

            def norm_gain(l, g, vectors):
                for m in range(vectors):
                    ins = nc.vector.scalar_tensor_tensor(gain[g][:, :, m], mod[l][:, 3 * g + 1, :, m], 1.0,
                                                         vecs[l][:, (V_N1, V_N2)[g]:(V_N1, V_N2)[g] + NT], ALU.add, ALU.mult)
                return ins

            def norm(l, tok, g, shift):
                rms(tok)
                parts = list(enumerate((LAT, CT)))[:1 + (tok > SEQ)]

                def finish(n):
                    dve.wait_ge(h_hi, n_hhi.up())
                    for m, cols in parts:
                        ins = nc.vector.scalar_tensor_tensor(Hlo[:, n, cols], tmp[:, n % 2, cols],
                                                             mod[l][:, shift, n, m:m + 1],
                                                             Hhi[:, n, cols].bitcast(F32), ALU.add, ALU.subtract)
                    ins.then_inc(h_ready, 1)

                for n in range(NT):
                    if n > 1:
                        dve.wait_ge(h_ready, n_hhi.now())
                    for m, cols in parts:
                        if n == 0:
                            dve.wait_ge(rstd_done, n_rstd.up())
                        ins = nc.vector.scalar_tensor_tensor(tmp[:, n % 2, cols], X[:, n, cols], gain[g][:, n, m:m + 1],
                                                             psS[:, RSTD][:, cols], ALU.mult, ALU.mult)
                    ins.then_inc(xn_ready, 1)
                    if n:
                        finish(n - 1)
                finish(NT - 1)

            def tmp_free(slot):
                dve.wait_ge(lat_read[1 - slot], n_slot[1 - slot].now())
                if n_ctx.begun():
                    dve.wait_ge(ctx_read, n_ctx.now())
                if n_qk.begun():
                    dve.wait_ge(qk_ready, n_qk.now())
                if n_y.begun():
                    dve.wait_ge(y_ready, n_y.now())

            def rotary(slot, ctx_too, next_nk):
                tmp_free(slot)
                n_qk.up()
                passed(slot, ctx_too, next_nk)
                dve.wait_ge(lat_done, n_lat.now())
                swapped, straight = tmp[:, 0, LAT], tmp[:, 1, LAT]
                link(nc.vector.stream_shuffle(swapped, psL[:, slot, :], HALF_SWAP))
                nc.vector.tensor_tensor(straight, psL[:, slot, :], cos, ALU.mult).then_inc(lat_read[slot], 1)
                link(nc.vector.tensor_tensor(swapped, swapped, sin, ALU.mult))
                if ctx_too:
                    dve.wait_ge(ctx_done, n_ctx.now())
                    nc.vector.tensor_copy(tmp[:, 1, CT], psC[:, 0:CTX]).then_inc(ctx_read, 1)
                nc.vector.tensor_tensor(straight, straight, swapped, ALU.add).then_inc(rotated, 1)

            def split_qk(l, u):
                w = TOK if with_ctx(u, l) else SEQ
                keys, i = u[0] in ("k", "ck"), u[1] % 2
                dve.wait_ge(qk_hi, n_qk.now())
                for m in range(2):
                    own, other = slice(m * 64, m * 64 + 64), slice(64 - m * 64, 128 - m * 64)
                    for to in (own, other) if keys else (other,):
                        ins = lo_part((KL if keys else QT)[i][to, m, 0:w], tmp[own, 1, 0:w],
                                      (KH if keys else QT)[i][own, m, 0:w])
                ins.then_inc(qk_ready, 1)

            def y_lo(l, n):
                w = width(l)
                dve.wait_ge(h_hi, n_hhi.up())
                nc.vector.scalar_tensor_tensor(Hlo[:, n, 0:w], Y[:, n, 0:w], 0.5, Hhi[:, n, 0:w].bitcast(F32),
                                               ALU.mult, ALU.subtract).then_inc(h_ready, 1)

            def branch(l, i, n, slot, next_nk):
                c, w = l < DEPTH - 1, width(l)
                tmp_free(slot)
                passed(slot, c, None)
                out = Y[:, n, :] if i == 0 else tmp[:, 1, :]
                dve.wait_ge(lat_done, n_lat.now())
                nc.vector.scalar_tensor_tensor(out[:, LAT], tmp[:, 0, LAT], 1.0, psL[:, slot, :],
                                               ALU.add, ALU.mult).then_inc(lat_read[slot], 1)
                if c:
                    dve.wait_ge(ctx_done, n_ctx.now())
                    nc.vector.scalar_tensor_tensor(out[:, CT], tmp[:, 0, CT], 1.0, psC[:, 0:CTX],
                                                   ALU.add, ALU.mult).then_inc(ctx_read, 1)
                if i:
                    dve.wait_ge(lat_read[slot], n_slot[slot].now())
                    if c:
                        dve.wait_ge(ctx_read, n_ctx.now())
                    nc.vector.tensor_tensor(Y[:, n, 0:w], Y[:, n, 0:w], tmp[:, 1, 0:w], ALU.add).then_inc(y_ready, 1)
                    n_y.up()
                split(slot, next_nk)

            def input_unit(l, u):
                kind, slot, c = u[0], PLACE[u] % 2, with_ctx(u, l)
                if kind in ("q", "k", "ck", "cq"):
                    rotary(slot, c, tiles_after(u))
                elif kind == "branch":
                    branch(l, u[1], u[2], slot, tiles_after(u))
                else:
                    passed(slot, c, tiles_after(u))
                if l == 0:
                    for _ in range(ADA_IN_UNIT.get(u, 0)):
                        ada_unit(0, ADA_PE + n_ada.now(), n_ada.now() % 4, 2)
                    if u == ("gate", 0, 0):
                        modulation(0, adasum[:, 2 * NT:3 * NT, :], 2, 3, 2)

            def row_max(l, kind, h, b):
                r = ROUND[l, (kind, h, b)]
                st = stat[r % 2]
                keys = key_blocks(kind, b)
                dve.wait_ge(scores_done, r)
                if kind == "C" and b < LBLK:
                    for k, kb in enumerate(keys[:-2]):
                        if kb != b:
                            area = maps[:, :, k * P:(k + 1) * P]
                            mask = (mask_prev if kb < b else mask_next).unsqueeze(1).broadcast_to([P, 2, P])
                            link(nc.vector.tensor_tensor(area, area, mask, ALU.add))
                link(nc.vector.reduce_max(st[:, MX:MX + 2], maps[:, :, 0:len(keys) * P], AX_X))
                if kind == "B":
                    nc.vector.tensor_scalar(st[:, NB:NB + 2], st[:, MX:MX + 2], -SCALE, None, ALU.mult).then_inc(bias_ready, 1)
                else:
                    link(nc.vector.scalar_tensor_tensor(st[:, NB:NB + 2], st[:, MX:MX + 2], -SCALE,
                                                        small[:, NEGSINK + 2 * h:NEGSINK + 2 * h + 2], ALU.mult, ALU.min))
                    nc.vector.tensor_tensor(st[:, SINKB:SINKB + 2], st[:, NB:NB + 2],
                                            small[:, NEGSINK + 2 * h:NEGSINK + 2 * h + 2],
                                            ALU.subtract).then_inc(bias_ready, 1)

            def normalise(l, kind, h, b):
                r = ROUND[l, (kind, h, b)]
                st, pr = stat[r % 2], prob[r % 2]
                n = len(key_blocks(kind, b)) * P
                dve.wait_ge(exp_done, r)
                if kind == "C":
                    link(nc.vector.tensor_tensor(st[:, SUM:SUM + 2], st[:, SUM:SUM + 2], st[:, SINKE:SINKE + 2], ALU.add))
                link(nc.vector.reciprocal(st[:, REC:REC + 2], st[:, SUM:SUM + 2]))
                if kind == "B":
                    nc.vector.tensor_tensor(st[:, REC + 1:REC + 2], st[:, REC + 1:REC + 2],
                                            small[:, NEGLAM:NEGLAM + 1], ALU.mult)
                    link(nc.vector.tensor_scalar(pr[:, 0, 0:n], pr[:, 0, 0:n], st[:, REC:REC + 1], None, ALU.mult))
                    nc.vector.scalar_tensor_tensor(pr[:, 0, 0:n], pr[:, 1, 0:n], st[:, REC + 1:REC + 2],
                                                   pr[:, 0, 0:n], ALU.mult, ALU.add).then_inc(prob_ready, 1)
                else:
                    for m in range(2):
                        ins = nc.vector.tensor_scalar(pr[:, m, 0:n], pr[:, m, 0:n], st[:, REC + m:REC + m + 1],
                                                      None, ALU.mult)
                    ins.then_inc(prob_ready, 1)

            def layernorm(l):
                nb = blocks_of(l)
                dve.wait_ge(t_read, FILL[l, "vn", KM - 1])
                for b in range(nb):
                    ins = nc.vector.bn_stats(bn[:, b, :], VN[:, b, :])
                link(ins)
                for b in range(nb):
                    ins = nc.vector.bn_aggr(small[:, LNMV + 2 * b:LNMV + 2 * b + 2], bn[:, b, :])
                ins.then_inc(ln_var, 1)
                dve.wait_ge(ln_std, l + 1)
                link(nc.vector.reciprocal(small[:, LNSTD:LNSTD + nb], small[:, LNSTD:LNSTD + nb]))
                for b in range(nb):
                    ins = nc.vector.tensor_scalar(VN[:, b, :], VN[:, b, :], small[:, LNMV + 2 * b:LNMV + 2 * b + 1],
                                                  small[:, LNSTD + b:LNSTD + b + 1], ALU.subtract, ALU.mult)
                ins.then_inc(ln_ready, 1)
                dve.wait_ge(ln_ready, l + 1)

            def mixers(l):
                nb, w = blocks_of(l), width(l)
                for step in STEPS[l]:
                    what, arg = step[0], step[1] if len(step) > 1 else None
                    fill = (l, *step)
                    if what == "unit":
                        input_unit(l, arg)
                    elif what == "rowsum":
                        dve.wait_ge(gating_loaded, 32 * (l + 1))
                        dve.wait_ge(t_done, FILL[fill])
                        for g in range(KM):
                            ins = nc.vector.scalar_tensor_tensor(bs_rows[:, g, :], psT[:, g * P:(g + 1) * P],
                                                                 vecs[l][:, V_LNB + g:V_LNB + g + 1], bs_rows[:, g, :],
                                                                 ALU.mult, ALU.add)
                        ins.then_inc(t_read, 1)
                    elif what == "split_qk":
                        split_qk(l, arg)
                    elif what == "vn":
                        dve.wait_ge(t_done, FILL[fill])
                        nc.vector.tensor_copy(VN[:, 0:nb, arg * P:(arg + 1) * P],
                                              psT[:, 0:nb * P].rearrange("p (b q) -> p b q", q=P)).then_inc(t_read, 1)
                    elif what == "ln":
                        layernorm(l)
                    elif what == "mix":
                        buf = mixed_buf[arg % 2][:, 0:w]
                        dve.wait_ge(t_done, FILL[fill])
                        if arg > 1:
                            dve.wait_ge(mixed_ready, KM * l + arg - 1)
                        nc.vector.scalar_tensor_tensor(buf.rearrange("p (b q) -> p b q", q=P),
                                                       psT[:, 0:w].rearrange("p (b q) -> p b q", q=P),
                                                       vecs[l][:, V_LNG + arg:V_LNG + arg + 1],
                                                       bs_rows[:, arg:arg + 1, :].broadcast_to([P, nb, P]),
                                                       ALU.mult, ALU.add).then_inc(t_read, 1)
                        dve.wait_ge(t_read, FILL[fill])
                        nc.vector.tensor_tensor(buf, buf, U[:, arg, 0:w], ALU.mult).then_inc(mixed, 1)
                        dve.wait_ge(mixed_hi, KM * l + arg + 1)
                        lo_part(Olo[:, arg, 0:w], buf, Ohi[:, arg, 0:w]).then_inc(mixed_ready, 1)
                    elif what == "scores":
                        row_max(l, *arg)
                    elif what == "norm":
                        normalise(l, *arg)
                    elif what == "out":
                        if arg[0] == "B" and arg[2] == nb - 1:
                            h = arg[1]
                            dve.wait_ge(head_std, HEADS_B * l + h + 1)
                            link(nc.vector.reciprocal(stat[0][:, HSTD:HSTD + nb], stat[0][:, HSTD:HSTD + nb]))
                            out = Otok[:, 0:nb, h * P:(h + 1) * P]
                            nc.vector.tensor_tensor(out, out, stat[0][:, HSTD:HSTD + nb].unsqueeze(2).broadcast_to(
                                [P, nb, P]), ALU.mult).then_inc(head_ready, 1)
                    elif what == "turn_out":
                        dve.wait_ge(o_hi, n_ohi.up())
                        nc.vector.scalar_tensor_tensor(Olo[:, arg, 0:w], psT[:, 0:w], small[:, SUBG:SUBG + 1],
                                                       Ohi[:, arg, 0:w].bitcast(F32), ALU.mult,
                                                       ALU.subtract).then_inc(t_read, 1)

            def x_tile(l, n, slot, gate, next_nk, squares, last=False):
                c = l < DEPTH - 1
                passed(slot, c, None if last else next_nk)
                dve.wait_ge(lat_done, n_lat.now())
                nc.vector.scalar_tensor_tensor(X[:, n, LAT], psL[:, slot, :], mod[l][:, gate, n, 0:1], X[:, n, LAT],
                                               ALU.mult, ALU.add).then_inc(lat_read[slot], 1)
                if c:
                    dve.wait_ge(ctx_done, n_ctx.now())
                    nc.vector.scalar_tensor_tensor(X[:, n, CT], psC[:, 0:CTX], mod[l][:, gate, n, 1:2], X[:, n, CT],
                                                   ALU.mult, ALU.add).then_inc(ctx_read, 1)
                if squares:
                    add_square(slot, width(l))
                if last and next_nk:
                    split(slot, next_nk)

            def ffn_tile(l, p, f, i, base, per_tile, next_nk):
                c = l < DEPTH - 1
                w = TOK + 1 if c else SEQ
                passed(0, c, next_nk)
                dve.wait_ge(lat_read[0], n_slot[0].now())
                if c:
                    dve.wait_ge(ctx_read, n_ctx.now())

                def tap(k):
                    return vecs[l][:, bass.ds(i + (V_CW + k * NF + f), 1)]
                link(nc.vector.tensor_scalar(conv[:, 0:w], apad[:, 1:w + 1], tap(1), tap(3), ALU.mult, ALU.add))
                link(nc.vector.scalar_tensor_tensor(conv[:, 0:w], apad[:, 0:w], tap(0), conv[:, 0:w], ALU.mult, ALU.add))
                nc.vector.scalar_tensor_tensor(conv[:, 0:w], apad[:, 2:w + 2], tap(2), conv[:, 0:w],
                                               ALU.mult, ALU.add).then_inc(conv_ready, 1)
                dve.wait_ge(th_ready, n_th.up())
                link(nc.vector.scalar_tensor_tensor(conv[:, 0:w], th[:, 0:w], 1.0, conv[:, 0:w], ALU.add, ALU.mult))
                if l == 0:
                    ada_unit(2, i * per_tile + base, 0, 2 if p == 0 else 1)
                passed(1, c, None)
                dve.wait_ge(lat_done, n_lat.now())
                nc.vector.scalar_tensor_tensor(tmp[:, 0, LAT], conv[:, 0:SEQ], 0.5, psL[:, 1, :],
                                               ALU.mult, ALU.mult).then_inc(lat_read[1], 1)
                if c:
                    dve.wait_ge(ctx_done, n_ctx.now())
                    nc.vector.scalar_tensor_tensor(tmp[:, 0, CT], conv[:, SEQ + 1:TOK + 1], 0.5, psC[:, 0:CTX],
                                                   ALU.mult, ALU.mult).then_inc(ctx_read, 1)
                dve.wait_ge(g_hi, n_ghi.up())
                wd = width(l)
                lo_part(Glo[:, i, 0:wd], tmp[:, 0, 0:wd], Ghi[:, i, 0:wd]).then_inc(g_ready, 1)
                split(1, next_nk)
                if l == 0 and per_tile == 2:
                    ada_unit(2, i * per_tile + (base + 1), 0, 1)

            link(nc.vector.memset(sqacc[:, :], 0.0))
            dve.wait_ge(condb_ready, 1)
            for u in range(ADA_PE, 2 * NT):
                ada_unit(0, u, n_ada.now() % 4, 2)
                if u == ADA_PE + 2:
                    for n in range(NT):
                        add_square(n % 2, TOK)
            for l in range(DEPTH):
                c = l < DEPTH - 1
                nb, w = blocks_of(l), width(l)
                lam_init = 0.8 - 0.6 * float(np.exp(-0.3 * l))
                if l == 0:
                    dve.wait_ge(ada_done, 1)
                    dve.wait_ge(vecs_loaded, 32)
                    nc.vector.tensor_copy(adasum[:, 0:ADA_PE, :], psT[:, 0:2 * ADA_PE].rearrange("p (u m) -> p u m", m=2)
                                          ).then_inc(ada_copied, 1)
                    dve.wait_ge(ada_copied, 1)
                    link(modulation(0, adasum[:, 0:2 * NT, :], 0, 2, 2))
                    norm_gain(0, 0, 2).then_inc(mod_ready, 1)
                    split(0, NT)
                    split(1, NT)
                norm(l, TOK, 0, 0)
                dve.wait_ge(lam_loaded, 32 * (l + 1))
                link(nc.vector.tensor_tensor(lamp[:, :, :], lamv[:, 0::2, :], lamv[:, 1::2, :], ALU.mult))
                nc.vector.reduce_sum(small[:, LAMSUM:LAMSUM + 2], lamp[:, :, :], AX_X).then_inc(lam_dot, 1)
                dve.wait_ge(lam_exp, l + 1)
                link(nc.vector.tensor_tensor(small[:, NEGLAM:NEGLAM + 1], small[:, LAMEXP + 1:LAMEXP + 2],
                                             small[:, LAMEXP:LAMEXP + 1], ALU.subtract))
                nc.vector.tensor_scalar(small[:, NEGLAM:NEGLAM + 1], small[:, NEGLAM:NEGLAM + 1], -lam_init, None, ALU.add)
                nc.vector.tensor_scalar(small[:, SUBG:SUBG + 1], vecs[l][:, V_SUB:V_SUB + 1], 1.0 - lam_init, None, ALU.mult)
                link(nc.vector.tensor_scalar(small[:, NEGSINK:NEGSINK + 8], small[:, SINK:SINK + 8], -1.0, None, ALU.mult))
                mixers(l)
                for h in range(PAIRS_C):
                    dve.wait_ge(oc_hi, KM * l + h + 1)
                    lo_part(Olo[:, h, 0:w], Ofeat[:, h, 0:w], Ohi[:, h, 0:w]).then_inc(oc_ready, 1)
                ada = {n_ada: 2, n_ada_slot[0]: 1, n_ada_slot[1]: 1, n_step: 4} if l == 0 else {}
                if l == 0:
                    dve.wait_ge(condb_ready, 2)
                with loop(dve, NT - 1, {n_hi: 2, n_lat: 2, n_ctx: 2 * c, n_slot[0]: 1, n_slot[1]: 1, n_y: 1} | ada) as n:
                    passed(0, c, NT)
                    branch(l, 2, n, 1, KM)
                    for s in range(2 if l == 0 else 0):
                        ada_unit(1, n * 2 + (ADA_START + s), s, 2)
                passed(0, c, NT)
                for n in range(3):
                    y_lo(l, n)
                branch(l, 2, NT - 1, 1, NT)
                for n in range(3, NT):
                    y_lo(l, n)
                link(nc.vector.memset(sqacc[:, :], 0.0))
                dve.wait_ge(x_back, 16 * (l + 1))
                per_pair = {n_hi: 2, n_lat: 2, n_ctx: 2 * c, n_slot[0]: 1, n_slot[1]: 1}
                with loop(dve, NT // 2 - 1, per_pair | {n_acc: 2} | ada) as i:
                    for s in range(2):
                        x_tile(l, 2 * i + s, s, 2, NT, True)
                        if l == 0:
                            ada_unit(1, i * 2 + (ADA_UNITS - NT + 2 + s), s, 2)
                x_tile(l, NT - 2, 0, 2, NT, True, True)
                if l == 0:
                    link(modulation(0, adasum[:, 3 * NT:ADA_UNITS, :], 3, 6, 2))
                    norm_gain(0, 1, 2)
                x_tile(l, NT - 1, 1, 2, NT, True, True)
                norm(l, w, 1, 3)
                link(nc.vector.memset(sqacc[:, :], 0.0))
                dve.wait_ge(pads_ready, l + 1)
                if l == 0:
                    dve.wait_ge(condb_ready, 3)
                for p, (f, tiles) in enumerate(PARTS):
                    vectors, per_tile = (2, 1) if p == 0 else (1, 2)
                    base = (0, 2 * NT, ADA_UNITS - 2 * tiles)[p]
                    with_x = (2, 1, 0)[p]

                    def ada_counts(n):
                        return {n_ada: n, n_ada_slot[0]: n, n_step: n * vectors} if l == 0 and n else {}
                    ffn_counts = per_pair | {n_th: 1, n_ghi: 1} | ada_counts(per_tile)
                    ffn_counts[n_step] = 3 + (2 if l == 0 else 0)
                    with loop(dve, tiles - 1, ffn_counts) as i:
                        ffn_tile(l, p, f, i, base, per_tile, NT)
                    ffn_tile(l, p, f, tiles - 1, base, per_tile, tiles)
                    base += tiles * per_tile
                    squares = p == len(PARTS) - 1
                    with loop(dve, NT // 2 - 1, per_pair | {n_acc: 2 * squares} | ada_counts(with_x)) as i:
                        for s in range(2):
                            x_tile(l, 2 * i + s, s, 5, tiles, squares)
                            if l == 0 and s < with_x:
                                ada_unit(2, i * with_x + (base + s), 0, vectors)
                    for n in (NT - 2, NT - 1):
                        x_tile(l, n, n % 2, 5, NT if l < DEPTH - 1 or not squares else None, squares, squares)
                        if l == 0 and n - (NT - 2) < with_x:
                            ada_unit(2, (NT // 2 - 1) * with_x + base + n - (NT - 2), 0, vectors)
                        if l == 0 and squares and n == NT - 2:
                            dve.wait_ge(vecs_loaded, 32)
                            modulation(1, adasum[:, 0:2 * NT, :], 0, 2, 2)
                            link(modulation(1, adasum[:, 2 * NT:ADA_UNITS, 0:1], 2, 6, 1))
                            norm_gain(1, 1, 1)
                            norm_gain(1, 0, 2).then_inc(mod_ready, 1)
            rms(SEQ)
            dve.wait_ge(rstd_done, n_rstd.up())
            for n in range(NT):
                nc.vector.scalar_tensor_tensor(X[:, n, LAT], X[:, n, LAT], final_gain[:, n:n + 1],
                                               psS[:, RSTD][:, LAT], ALU.mult, ALU.mult).then_inc(fin_ready, 1)


def constant_table():
    table = np.zeros((P, C_END), np.float32)
    half = HEAD_DIM // 2
    inv = (np.float32(ROPE_BASE) ** (-np.arange(0, half, 2, dtype=np.float32) / np.float32(half))).astype(np.float32)
    place = np.arange(SEQ)
    for p in range(P):
        axis = place // GRID_W if (p % HEAD_DIM) < half else place % GRID_W
        angle = axis.astype(np.float32) * inv[p % 16]
        table[p, C_COS:C_COS + SEQ] = np.cos(angle)
        table[p, C_SIN:C_SIN + SEQ] = np.sin(angle) * (-1 if p % 32 < 16 else 1)
    table[:, C_ID:C_ID + P] = np.eye(P)
    q, k = np.arange(P)[:, None], np.arange(P)[None, :]
    table[:, C_PREV:C_PREV + P] = np.where(k >= q, 0, NEG_INF)
    table[:, C_NEXT:C_NEXT + P] = np.where(k <= q, 0, NEG_INF)
    return table


def input_columns():
    start = {"u": 0, "a": MIX_W, "q": 2 * MIX_W, "k": 3 * MIX_W, "v": 4 * MIX_W, "ck": 6 * MIX_W, "cv": 6 * MIX_W + P}
    cols = []
    for kind, i in KINDS:
        if kind == "cq":
            cols += [np.arange(HEAD_DIM) + 5 * MIX_W + (g * PAIRS_C + i) * HEAD_DIM for g in range(2)]
        else:
            cols.append(np.arange(P) + start[kind] + i * P)
    return np.concatenate(cols + [np.arange(N_BRANCH * D_MODEL) + 6 * MIX_W + 2 * P])


def units(w):
    d, k, n = w.shape
    return np.ascontiguousarray(w.reshape(d, k // P, P, n // P, P).transpose(0, 3, 2, 1, 4)).reshape(d, n // P, P, k)


def per_feature(v):
    return np.ascontiguousarray(np.swapaxes(v.reshape(*v.shape[:-1], -1, P), -1, -2))


def laid_out(i):
    i = {k: np.asarray(v) for k, v in i.items()}
    rows = np.arange(MIX_W).reshape(2, PAIRS_C, HEAD_DIM).transpose(1, 0, 2).reshape(-1)
    branch = np.stack([i["w_branch"][:, 0], i["w_branch"][:, 1], i["w_branch"][:, 2][:, rows]], 1)
    cw = i["conv_w"]
    return {
        "x": per_feature(i["x"][0]).transpose(1, 2, 0), "ctx": per_feature(i["ctx"][0]).transpose(1, 2, 0),
        "c": per_feature(i["c"][0]), "c_ctx": per_feature(i["c_ctx"]),
        "c_row": i["c"].reshape(-1), "c_ctx_row": i["c_ctx"].reshape(-1),
        "w_ada_first": units(i["w_ada"][:1, :, :ADA_PE * P])[0].transpose(1, 0, 2),
        "w_ada_rows": i["w_ada"].transpose(0, 2, 1).reshape(DEPTH, ADA_UNITS, P, D_MODEL),
        "w_in": units(i["w_in"][:, :, input_columns()]),
        "w_branch": np.concatenate([units(branch[:, n]) for n in range(N_BRANCH)], 1),
        "w_out": units(i["w_out"]), "w_gate": units(i["w_gate"]), "w_up": units(i["w_up"]),
        "w_down": units(i["w_down"]),
        "vecs": np.concatenate([per_feature(v) for v in (
            i["b_ada"], i["norm1_g"], i["norm2_g"], i["diff_subln_g"], cw[:, 0], cw[:, 1], cw[:, 2], i["conv_b"],
            i["sgu_ln_g"], i["sgu_ln_b"])], -1),
        "lam": np.stack([i[n] for n in ("lam_q1", "lam_k1", "lam_q2", "lam_k2")], 1),
        "sinks": i["sinks"].reshape(DEPTH, 2, PAIRS_C).transpose(0, 2, 1).reshape(DEPTH, -1),
        "w_s": i["w_s"].transpose(0, 3, 1, 2), "b_s": i["b_s"], "final_g": per_feature(i["final_g"]),
        "consts": constant_table(),
    }


def kernel(**inputs):
    import concourse.bacc as bacc
    from concourse.bass_utils import run_bass_kernel_spmd

    nc = bacc.Bacc("TRN2", target_bir_lowering=False, num_devices=1)
    arrays, tensors = {}, {}
    for name, a in laid_out(inputs).items():
        arrays[f"in_{name}"] = np.ascontiguousarray(a)
        tensors[name] = nc.dram_tensor(f"in_{name}", a.shape, mybir.dt.from_np(a.dtype), kind="ExternalInput").ap()
    tensors["out"] = nc.dram_tensor("out", (P, NT, SEQ), F32, kind="ExternalOutput").ap()
    hybrid_prefix_dit_block(nc, tensors)
    result = run_bass_kernel_spmd(nc, [arrays], core_ids=[0]).results[0]["out"]
    return np.ascontiguousarray(result.transpose(2, 1, 0)).reshape(1, SEQ, D_MODEL)
```
